# Optimizing a Trainium2 kernel written in Bass

```python
import math
import jax
import jax.numpy as jnp
from jax import lax
import numpy as np

D_MODEL = 1024
BATCH = 1
SEQ = 1024
DEPTH = 1

CTX_LEN = 256
GRID_W = 64
ROPE_BASE = 10000.0
NORM_EPS = 1e-6
NEG_INF = -1e30
Q_BLOCK = 128
HEAD_DIM = 64

SWA_HEADS = 4
SWA_KV_HEADS = 2
SWA_WINDOW = 128
SWA_BLOCK = 128
DIFF_HEADS = 4
DIFF_QK_DIM = 32
DIFF_V_DIM = 64
RET_HEADS = 4
RET_K_DIM = 64
RET_V_DIM = 64
RET_CHUNK = 128
MLA_HEADS = 4
MLA_Q_LORA = 256
MLA_KV_LORA = 128
MLA_NOPE_DIM = 64
MLA_ROPE_DIM = 32
MLA_V_DIM = 64

SWA_IN = SWA_HEADS * HEAD_DIM + 2 * SWA_KV_HEADS * HEAD_DIM
DIFF_IN = 2 * (DIFF_HEADS * 2 * DIFF_QK_DIM) + DIFF_HEADS * DIFF_V_DIM
RET_IN = 2 * RET_HEADS * RET_K_DIM + 2 * RET_HEADS * RET_V_DIM
MLA_IN = MLA_Q_LORA + MLA_KV_LORA + MLA_ROPE_DIM
D_IN = SWA_IN + DIFF_IN + RET_IN + MLA_IN
D_MIX = SWA_HEADS * HEAD_DIM + DIFF_HEADS * DIFF_V_DIM + RET_HEADS * RET_V_DIM + MLA_HEADS * MLA_V_DIM

MOE_GROUPS = 4
MOE_EXPERTS_PER_GROUP = 8
MOE_EXPERTS = MOE_GROUPS * MOE_EXPERTS_PER_GROUP
MOE_TOP_K = 2
MOE_HIDDEN = 512
MOE_BLOCK = 128

kernel_name = "hybrid_parallel_heads_hmoe_dit"

def rms_norm(x, g):
    xf = x.astype(jnp.float32)
    y = xf * lax.rsqrt(jnp.mean(xf * xf, axis=-1, keepdims=True) + NORM_EPS)
    return (y * g.astype(jnp.float32)).astype(x.dtype)

def modulate(h, shift, scale):
    return h * (1.0 + scale) + shift

def axial_rope(x, row, col):
    r = x.shape[-1]
    nf = r // 4
    inv = 1.0 / (ROPE_BASE ** (jnp.arange(nf, dtype=jnp.float32) / nf))

    def rot(xh, pos):
        ang = pos.astype(jnp.float32)[:, None] * inv[None, :]
        cos = jnp.cos(ang)[None, :, None, :]
        sin = jnp.sin(ang)[None, :, None, :]
        x1 = xh[..., :nf].astype(jnp.float32)
        x2 = xh[..., nf:].astype(jnp.float32)
        return jnp.concatenate([x1 * cos - x2 * sin, x1 * sin + x2 * cos], axis=-1)

    out = jnp.concatenate([rot(x[..., :2 * nf], row), rot(x[..., 2 * nf:], col)], axis=-1)
    return out.astype(x.dtype)

def swa_mixer(z, zc, sink, row, col, need_ctx):
    B, T, _ = z.shape
    Tc = zc.shape[1]
    G, R, d = SWA_KV_HEADS, SWA_HEADS // SWA_KV_HEADS, HEAD_DIM
    qw, kw = SWA_HEADS * d, G * d
    scale = d ** -0.5

    def split(u):
        b, t = u.shape[:2]
        return (u[..., :qw].reshape(b, t, SWA_HEADS, d),
                u[..., qw:qw + kw].reshape(b, t, G, d),
                u[..., qw + kw:].reshape(b, t, G, d))

    q, k, v = split(z)
    qc, kc, vc = split(zc)
    q = (axial_rope(q, row, col) * scale).reshape(B, T, G, R, d)
    k = axial_rope(k, row, col)
    sink_gr = sink.astype(jnp.float32).reshape(G, R)

    Lb = SWA_BLOCK
    nb = T // Lb
    nk = 3 * Lb
    qb = q.reshape(B, nb, Lb, G, R, d)

    def band(a):
        ap = jnp.pad(a, ((0, 0), (Lb, Lb), (0, 0), (0, 0))).reshape(B, nb + 2, Lb, G, d)
        return jnp.concatenate([ap[:, :-2], ap[:, 1:-1], ap[:, 2:]], axis=2)

    kb, vb = band(k), band(v)
    blk = jnp.arange(nb, dtype=jnp.int32)
    qpos = blk[:, None, None] * Lb + jnp.arange(Lb, dtype=jnp.int32)[None, :, None]
    kpos = (blk[:, None, None] - 1) * Lb + jnp.arange(nk, dtype=jnp.int32)[None, None, :]
    valid = (jnp.abs(qpos - kpos) <= SWA_WINDOW) & (kpos >= 0) & (kpos < T)
    s_band = jnp.where(valid[None, :, None, None],
                       jnp.einsum('bnqgrd,bnkgd->bngrqk', qb, kb).astype(jnp.float32), NEG_INF)
    s_ctx = jnp.einsum('bnqgrd,bcgd->bngrqc', qb, kc).astype(jnp.float32)
    s_sink = jnp.broadcast_to(sink_gr[None, None, :, :, None, None], (B, nb, G, R, Lb, 1))
    p = jax.nn.softmax(jnp.concatenate([s_band, s_ctx, s_sink], axis=-1), axis=-1)
    o = (jnp.einsum('bngrqk,bnkgd->bnqgrd', p[..., :nk].astype(vb.dtype), vb)
         + jnp.einsum('bngrqc,bcgd->bnqgrd', p[..., nk:nk + Tc].astype(vc.dtype), vc))
    y = o.reshape(B, T, SWA_HEADS * d)

    yc = None
    if need_ctx:
        qcs = qc.reshape(B, Tc, G, R, d) * scale
        sc = jnp.einsum('bqgrd,bcgd->bgrqc', qcs, kc).astype(jnp.float32)
        sc_sink = jnp.broadcast_to(sink_gr[None, :, :, None, None], (B, G, R, Tc, 1))
        pc = jax.nn.softmax(jnp.concatenate([sc, sc_sink], axis=-1), axis=-1)
        yc = jnp.einsum('bgrqc,bcgd->bqgrd', pc[..., :Tc].astype(vc.dtype), vc).reshape(B, Tc, SWA_HEADS * d)
    return y, yc

def diff_mixer(z, zc, lam_p, subln_g, lambda_init, row, col, need_ctx):
    B, T, _ = z.shape
    Tc = zc.shape[1]
    H, dq, dv = DIFF_HEADS, DIFF_QK_DIM, DIFF_V_DIM
    qw = H * 2 * dq
    scale = dq ** -0.5

    def split(u):
        b, t = u.shape[:2]
        return (u[..., :qw].reshape(b, t, 2 * H, dq),
                u[..., qw:2 * qw].reshape(b, t, 2 * H, dq),
                u[..., 2 * qw:].reshape(b, t, H, dv))

    q, k, v = split(z)
    qc, kc, vc = split(zc)
    q = axial_rope(q, row, col).reshape(B, T, H, 2, dq) * scale
    k = axial_rope(k, row, col).reshape(B, T, H, 2, dq)
    kc = kc.reshape(B, Tc, H, 2, dq)
    lp = lam_p.astype(jnp.float32)
    lam = jnp.exp(jnp.sum(lp[0] * lp[1])) - jnp.exp(jnp.sum(lp[2] * lp[3])) + lambda_init

    def attend(qb, kk, vv):
        s = jnp.einsum('bqhmd,bkhmd->bhmqk', qb, kk).astype(jnp.float32)
        p = jax.nn.softmax(s, axis=-1)
        a = p[:, :, 0] - lam * p[:, :, 1]
        return jnp.einsum('bhqk,bkhe->bqhe', a.astype(vv.dtype), vv)

    def finish(o):
        b, t = o.shape[:2]
        return (rms_norm(o, subln_g) * (1.0 - lambda_init)).reshape(b, t, H * dv)

    k_all = jnp.concatenate([kc, k], axis=1)
    v_all = jnp.concatenate([vc, v], axis=1)
    nb = T // Q_BLOCK
    qblocks = jnp.moveaxis(q.reshape(B, nb, Q_BLOCK, H, 2, dq), 1, 0)
    o = lax.map(lambda qb: attend(qb, k_all, v_all), qblocks)
    y = finish(jnp.moveaxis(o, 0, 1).reshape(B, T, H, dv))

    yc = None
    if need_ctx:
        yc = finish(attend(qc.reshape(B, Tc, H, 2, dq) * scale, kc, vc))
    return y, yc

def retention_final_state(k, v, lg):
    T = k.shape[1]
    w = jnp.exp((T - 1 - jnp.arange(T, dtype=jnp.float32))[:, None] * lg[None, :])
    return jnp.einsum('bthd,bthe->bhde', k.astype(jnp.float32) * w[None, :, :, None], v.astype(jnp.float32))

def retention_chunkwise(q, k, v, s0, lg):
    B, T, H, _ = q.shape
    dv = v.shape[-1]
    L = RET_CHUNK
    n = T // L
    i = jnp.arange(L, dtype=jnp.float32)
    rel = i[:, None] - i[None, :]
    inner_decay = jnp.where(rel[None] >= 0, jnp.exp(jnp.maximum(rel, 0.0)[None] * lg[:, None, None]), 0.0)
    q_decay = jnp.exp((i[:, None] + 1.0) * lg[None, :])
    k_decay = jnp.exp((L - 1.0 - i)[:, None] * lg[None, :])
    chunk_decay = jnp.exp(L * lg)

    def to_chunks(a):
        return jnp.moveaxis(a.astype(jnp.float32).reshape(B, n, L, H, a.shape[-1]), 1, 0)

    def step(s, xs):
        qc, kc, vc = xs
        a = jnp.einsum('blhd,bmhd->bhlm', qc, kc) * inner_decay[None]
        o = jnp.einsum('bhlm,bmhe->blhe', a, vc)
        o = o + jnp.einsum('blhd,bhde->blhe', qc * q_decay[None, :, :, None], s)
        s = s * chunk_decay[None, :, None, None] + jnp.einsum('bmhd,bmhe->bhde', kc * k_decay[None, :, :, None], vc)
        return s, o

    s, o = lax.scan(step, s0, (to_chunks(q), to_chunks(k), to_chunks(v)))
    return s, jnp.moveaxis(o, 0, 1).reshape(B, T, H, dv)

def gated_group_norm(o, g, gn_g, dtype):
    of = o.astype(jnp.float32)
    mu = jnp.mean(of, axis=-1, keepdims=True)
    var = jnp.mean(jnp.square(of - mu), axis=-1, keepdims=True)
    on = ((of - mu) * lax.rsqrt(var + NORM_EPS)).reshape(o.shape[0], o.shape[1], -1)
    return (on * gn_g.astype(jnp.float32) * jax.nn.silu(g.astype(jnp.float32))).astype(dtype)

def retention_mixer(z, zc, decay_logit, gn_g, row, col, need_ctx):
    B, T, _ = z.shape
    Tc = zc.shape[1]
    H, dk, dv = RET_HEADS, RET_K_DIM, RET_V_DIM
    qw, vw = H * dk, H * dv
    scale = dk ** -0.5

    def split(u):
        b, t = u.shape[:2]
        return (u[..., :qw].reshape(b, t, H, dk), u[..., qw:2 * qw].reshape(b, t, H, dk),
                u[..., 2 * qw:2 * qw + vw].reshape(b, t, H, dv), u[..., 2 * qw + vw:])

    q, k, v, g = split(z)
    qc, kc, vc, gc = split(zc)
    q = axial_rope(q, row, col) * scale
    k = axial_rope(k, row, col)
    log_gamma = jax.nn.log_sigmoid(decay_logit.astype(jnp.float32))

    outs, outs_c = [], []
    for direction in range(2):
        lg = log_gamma[direction]
        fl = (lambda a: jnp.flip(a, axis=1)) if direction == 1 else (lambda a: a)
        if need_ctx:
            s_ctx, oc = retention_chunkwise(fl(qc * scale), fl(kc), fl(vc),
                                            jnp.zeros((B, H, dk, dv), jnp.float32), lg)
            outs_c.append(fl(oc))
        else:
            s_ctx = retention_final_state(fl(kc), fl(vc), lg)
        _, o = retention_chunkwise(fl(q), fl(k), fl(v), s_ctx, lg)
        outs.append(fl(o))

    y = gated_group_norm(outs[0] + outs[1], g, gn_g, z.dtype)
    yc = gated_group_norm(outs_c[0] + outs_c[1], gc, gn_g, zc.dtype) if need_ctx else None
    return y, yc

def mla_mixer(z, zc, q_norm_g, w_uq, kv_norm_g, w_ukv, row, col, need_ctx):
    B, T, _ = z.shape
    Tc = zc.shape[1]
    H, dn, dr, dv = MLA_HEADS, MLA_NOPE_DIM, MLA_ROPE_DIM, MLA_V_DIM
    scale = (dn + dr) ** -0.5

    def proj_q(u):
        b, t = u.shape[:2]
        qq = (rms_norm(u[..., :MLA_Q_LORA], q_norm_g) @ w_uq).reshape(b, t, H, dn + dr)
        return qq[..., :dn] * scale, qq[..., dn:] * scale

    def proj_kv(u):
        b, t = u.shape[:2]
        kv = (rms_norm(u[..., MLA_Q_LORA:MLA_Q_LORA + MLA_KV_LORA], kv_norm_g) @ w_ukv).reshape(b, t, H, dn + dv)
        return kv[..., :dn], kv[..., dn:], u[..., MLA_Q_LORA + MLA_KV_LORA:]

    qn, qr = proj_q(z)
    qr = axial_rope(qr, row, col)
    kn, v, kr = proj_kv(z)
    kr = axial_rope(kr[:, :, None, :], row, col)[:, :, 0]
    kcn, vc, kcr = proj_kv(zc)

    def attend(qn_b, qr_b, kn_, kr_, v_):
        s = (jnp.einsum('bqhd,bkhd->bhqk', qn_b, kn_)
             + jnp.einsum('bqhr,bkr->bhqk', qr_b, kr_)).astype(jnp.float32)
        p = jax.nn.softmax(s, axis=-1)
        return jnp.einsum('bhqk,bkhe->bqhe', p.astype(v_.dtype), v_)

    kn_all = jnp.concatenate([kcn, kn], axis=1)
    kr_all = jnp.concatenate([kcr, kr], axis=1)
    v_all = jnp.concatenate([vc, v], axis=1)
    nb = T // Q_BLOCK
    qn_b = jnp.moveaxis(qn.reshape(B, nb, Q_BLOCK, H, dn), 1, 0)
    qr_b = jnp.moveaxis(qr.reshape(B, nb, Q_BLOCK, H, dr), 1, 0)
    o = lax.map(lambda a: attend(a[0], a[1], kn_all, kr_all, v_all), (qn_b, qr_b))
    y = jnp.moveaxis(o, 0, 1).reshape(B, T, H * dv)

    yc = None
    if need_ctx:
        qcn, qcr = proj_q(zc)
        yc = attend(qcn, qcr, kcn, kcr, vc).reshape(B, Tc, H * dv)
    return y, yc

def grouped_experts(x, e_idx, e_w, w_gate, w_up, w_down):
    N, D = x.shape
    E, K, Lb = MOE_EXPERTS, e_idx.shape[1], MOE_BLOCK
    M = N * K
    flat_e = e_idx.reshape(-1).astype(jnp.int32)
    flat_tok = jnp.arange(M, dtype=jnp.int32) // K
    flat_w = e_w.reshape(-1)
    order = jnp.argsort(flat_e)
    se = flat_e[order]
    counts = jnp.bincount(flat_e, length=E).astype(jnp.int32)
    padded = (counts + Lb - 1) // Lb * Lb
    start = jnp.cumsum(counts) - counts
    pend = jnp.cumsum(padded)
    pstart = pend - padded
    dest = pstart[se] + jnp.arange(M, dtype=jnp.int32) - start[se]
    n_blocks = (M + E * (Lb - 1) + Lb - 1) // Lb
    cap = n_blocks * Lb
    buf_tok = jnp.zeros((cap,), jnp.int32).at[dest].set(flat_tok[order])
    buf_w = jnp.zeros((cap,), x.dtype).at[dest].set(flat_w[order].astype(x.dtype))
    block_e = jnp.minimum(jnp.searchsorted(pend, jnp.arange(n_blocks, dtype=jnp.int32) * Lb, side='right'), E - 1)
    xb = x[buf_tok].reshape(n_blocks, Lb, D)

    def run(args):
        xblk, e = args
        return (jax.nn.silu(xblk @ w_gate[e]) * (xblk @ w_up[e])) @ w_down[e]

    yb = lax.map(run, (xb, block_e)).reshape(cap, D)
    return jnp.zeros_like(x).at[buf_tok].add(yb * buf_w[:, None])

def hier_moe(x, w_group, b_group, w_expert, b_expert, w_gate, w_up, w_down):
    N = x.shape[0]
    rows = jnp.arange(N)
    g_logits = (x @ w_group + b_group).astype(jnp.float32)
    g_prob = jax.nn.softmax(g_logits, axis=-1)
    g_idx = jnp.argmax(g_logits, axis=-1)
    g_w = g_prob[rows, g_idx]
    e_logits = (x @ w_expert + b_expert).astype(jnp.float32).reshape(N, MOE_GROUPS, MOE_EXPERTS_PER_GROUP)
    e_logits = e_logits[rows, g_idx]
    top_val, top_loc = lax.top_k(e_logits, MOE_TOP_K)
    e_w = jax.nn.softmax(top_val, axis=-1) * g_w[:, None]
    e_idx = g_idx[:, None] * MOE_EXPERTS_PER_GROUP + top_loc
    return grouped_experts(x, e_idx, e_w, w_gate, w_up, w_down)

def trunk_layer(x, xc, c_act, cc_act, row, col, layer_idx, need_ctx,
                w_mod, b_mod, norm1_g, norm2_g, w_in, w_out, swa_sink, diff_lambda, diff_subln_g,
                ret_decay_logit, ret_gn_g, mla_q_norm_g, mla_w_uq, mla_kv_norm_g, mla_w_ukv,
                moe_w_group, moe_b_group, moe_w_expert, moe_b_expert, moe_w_gate, moe_w_up, moe_w_down):
    B, T, D = x.shape
    Tc = xc.shape[1]
    sh1, sc1, g1, sh2, sc2, g2 = jnp.split(c_act @ w_mod + b_mod, 6, axis=-1)
    csh1, csc1, cg1, csh2, csc2, cg2 = jnp.split(cc_act @ w_mod + b_mod, 6, axis=-1)

    h = modulate(rms_norm(x, norm1_g), sh1[:, None], sc1[:, None])
    hc = modulate(rms_norm(xc, norm1_g), csh1, csc1)
    z = h @ w_in
    zc = hc @ w_in
    o1, o2, o3 = SWA_IN, SWA_IN + DIFF_IN, SWA_IN + DIFF_IN + RET_IN
    lambda_init = 0.8 - 0.6 * math.exp(-0.3 * layer_idx)

    ya, yac = swa_mixer(z[..., :o1], zc[..., :o1], swa_sink, row, col, need_ctx)
    yb, ybc = diff_mixer(z[..., o1:o2], zc[..., o1:o2], diff_lambda, diff_subln_g, lambda_init, row, col, need_ctx)
    yr, yrc = retention_mixer(z[..., o2:o3], zc[..., o2:o3], ret_decay_logit, ret_gn_g, row, col, need_ctx)
    ym, ymc = mla_mixer(z[..., o3:], zc[..., o3:], mla_q_norm_g, mla_w_uq, mla_kv_norm_g, mla_w_ukv, row, col, need_ctx)

    x = x + g1[:, None] * (jnp.concatenate([ya, yb, yr, ym], axis=-1) @ w_out)
    h2 = modulate(rms_norm(x, norm2_g), sh2[:, None], sc2[:, None])
    moe_args = (moe_w_group, moe_b_group, moe_w_expert, moe_b_expert, moe_w_gate, moe_w_up, moe_w_down)
    if need_ctx:
        xc = xc + cg1 * (jnp.concatenate([yac, ybc, yrc, ymc], axis=-1) @ w_out)
        h2c = modulate(rms_norm(xc, norm2_g), csh2, csc2)
        m = hier_moe(jnp.concatenate([h2.reshape(-1, D), h2c.reshape(-1, D)], axis=0), *moe_args)
        x = x + g2[:, None] * m[:B * T].reshape(B, T, D)
        xc = xc + cg2 * m[B * T:].reshape(B, Tc, D)
    else:
        x = x + g2[:, None] * hier_moe(h2.reshape(-1, D), *moe_args).reshape(B, T, D)
    return x, xc

def setup_inputs(seed: int = 0) -> dict:
    key = jax.random.key(seed)
    ks = iter(jax.random.split(key, 32))
    f32 = jnp.float32
    L, D = DEPTH, D_MODEL

    def nrm(shape, scale):
        return jax.random.normal(next(ks), shape, f32) * scale

    ret_logit0 = jnp.log(2.0 ** (5.0 + jnp.arange(RET_HEADS, dtype=f32)) - 1.0)
    return {
        "x": nrm((BATCH, SEQ, D), 1.0),
        "c": nrm((BATCH, D), 1.0),
        "ctx": nrm((BATCH, CTX_LEN, D), 1.0),
        "c_ctx": nrm((D,), 1.0),
        "w_mod": nrm((L, D, 6 * D), 0.5 * D ** -0.5),
        "b_mod": nrm((L, 6 * D), 0.02),
        "norm1_g": 1.0 + nrm((L, D), 0.02),
        "norm2_g": 1.0 + nrm((L, D), 0.02),
        "w_in": nrm((L, D, D_IN), D ** -0.5),
        "w_out": nrm((L, D_MIX, D), D_MIX ** -0.5),
        "swa_sink": nrm((L, SWA_HEADS), 0.5),
        "diff_lambda": nrm((L, 4, DIFF_QK_DIM), 0.1),
        "diff_subln_g": 1.0 + nrm((L, DIFF_V_DIM), 0.02),
        "ret_decay_logit": ret_logit0[None, None, :] + nrm((L, 2, RET_HEADS), 0.1),
        "ret_gn_g": 1.0 + nrm((L, RET_HEADS * RET_V_DIM), 0.02),
        "mla_q_norm_g": 1.0 + nrm((L, MLA_Q_LORA), 0.02),
        "mla_w_uq": nrm((L, MLA_Q_LORA, MLA_HEADS * (MLA_NOPE_DIM + MLA_ROPE_DIM)), MLA_Q_LORA ** -0.5),
        "mla_kv_norm_g": 1.0 + nrm((L, MLA_KV_LORA), 0.02),
        "mla_w_ukv": nrm((L, MLA_KV_LORA, MLA_HEADS * (MLA_NOPE_DIM + MLA_V_DIM)), MLA_KV_LORA ** -0.5),
        "moe_w_group": nrm((L, D, MOE_GROUPS), D ** -0.5),
        "moe_b_group": nrm((L, MOE_GROUPS), 0.01),
        "moe_w_expert": nrm((L, D, MOE_EXPERTS), D ** -0.5),
        "moe_b_expert": nrm((L, MOE_EXPERTS), 0.01),
        "moe_w_gate": nrm((L, MOE_EXPERTS, D, MOE_HIDDEN), D ** -0.5),
        "moe_w_up": nrm((L, MOE_EXPERTS, D, MOE_HIDDEN), D ** -0.5),
        "moe_w_down": nrm((L, MOE_EXPERTS, MOE_HIDDEN, D), MOE_HIDDEN ** -0.5),
        "final_norm_g": 1.0 + nrm((D,), 0.02),
    }

def reference(x, c, ctx, c_ctx, w_mod, b_mod, norm1_g, norm2_g, w_in, w_out, swa_sink, diff_lambda,
              diff_subln_g, ret_decay_logit, ret_gn_g, mla_q_norm_g, mla_w_uq, mla_kv_norm_g, mla_w_ukv,
              moe_w_group, moe_b_group, moe_w_expert, moe_b_expert, moe_w_gate, moe_w_up, moe_w_down,
              final_norm_g):
    T = x.shape[1]
    ROWS = T // GRID_W
    row = jnp.repeat(jnp.arange(ROWS, dtype=jnp.int32), GRID_W)
    col = jnp.tile(jnp.arange(GRID_W, dtype=jnp.int32), ROWS)
    c_act = jax.nn.silu(c)
    cc_act = jax.nn.silu(c_ctx)
    xc = ctx
    for l in range(DEPTH):
        x, xc = trunk_layer(
            x, xc, c_act, cc_act, row, col, l, l < DEPTH - 1,
            w_mod[l], b_mod[l], norm1_g[l], norm2_g[l], w_in[l], w_out[l], swa_sink[l], diff_lambda[l],
            diff_subln_g[l], ret_decay_logit[l], ret_gn_g[l], mla_q_norm_g[l], mla_w_uq[l], mla_kv_norm_g[l],
            mla_w_ukv[l], moe_w_group[l], moe_b_group[l], moe_w_expert[l], moe_b_expert[l], moe_w_gate[l],
            moe_w_up[l], moe_w_down[l])
    return rms_norm(x, final_norm_g)


_drawn_inputs = setup_inputs


def setup_inputs(seed=0):
    import zlib

    import numpy as np

    out = dict(_drawn_inputs(seed))
    spreads = {}
    factors = {'norm1_g': 8.0,
     'norm2_g': 4.834,
     'swa_sink': 8.0,
     'diff_lambda': 3.612,
     'diff_subln_g': 61.923,
     'ret_gn_g': 8.0,
     'mla_q_norm_g': 8.0,
     'mla_w_uq': 3.574,
     'mla_kv_norm_g': 8.0,
     'moe_b_group': 8.0,
     'moe_b_expert': 27.284,
     'final_norm_g': 22.218}
    for name, (base, spread) in spreads.items():
        noise = np.random.default_rng([zlib.crc32(name.encode()), seed]).standard_normal(out[name].shape)
        drawn = base * np.exp(spread * noise) if base else spread * noise
        out[name] = jnp.asarray(drawn.astype(out[name].dtype))
    for name, factor in factors.items():
        out[name] = (out[name] * factor).astype(out[name].dtype)
    return out
```

```python
from contextlib import ExitStack

import concourse.bass as bass
import numpy as np
from concourse import mybir

F32 = mybir.dt.float32
I32 = mybir.dt.int32
U32 = mybir.dt.uint32
ALU = mybir.AluOpType
ACT = mybir.ActivationFunctionType
AX = mybir.AxisListType
ds = bass.ds

P = 128
D = 1024
KD = D // P
SEQ, CTX = 1024, 256
NLAT, NCTX = SEQ // P, CTX // P
NTOK = NLAT + NCTX
GRID_W = 64
EPS = 1e-6
NEG = -1e30
WINDOW = 128
DIN = 2720
LAMBDA_INIT = 0.2
EXPERTS, GROUPS, PER_GROUP, HIDDEN = 32, 4, 8, 512
HB = HIDDEN // P
NOVER = 2 * SEQ // P - 1
MOD_GROUPS = 6 * D // 512
NBLK = EXPERTS + NOVER + 2

Z_KVL, Z_KR, Z_QL, Z_SK, Z_RK, Z_SQ, Z_RQ, Z_DK, Z_DQ, Z_SV, Z_DV, Z_RV, Z_G = (
    0, 128, 160, 416, 544, 800, 1056, 1312, 1568, 1824, 1952, 2208, 2464)
CHUNKS = [(0, 416, 160), (416, 384, 384), (800, 512, 0), (1312, 512, 256), (1824, 384, 384), (2208, 512, 256)]
K_D, K_S, V_S, V_D, V_M, K_M, R_U, KVW = 0, 256, 384, 512, 768, 1024, 1536, 1792
Q_S, Q_D, Q_M, Q_R, K_R, Q_FB, V_R, GATE, QW = 0, 256, 512, 1024, 1280, 1536, 2048, 2304, 2560
PACKW = KVW + QW

C_C, C_CTX, C_BMOD, C_N1, C_N2, C_QG, C_KVG, C_END = 0, 8, 16, 64, 72, 80, 82, 83
W_SUBLN, W_GN, W_SINK, W_DECAY, W_LAM, W_RB, W_FN, W_END = 0, 64, 320, 324, 332, 460, 496, 1520
T_C64, T_S64, T_N64, T_C32, T_S32, T_N32, T_END = 0, 64, 96, 128, 160, 176, 192
I_ID, I_REL, I_RELB, I_MF, I_MB, I_TRI, I_STEP, I_E32, I_G4, I_END = (
    0, 128, 256, 384, 512, 640, 768, 772, 804, 808)


class Tile:

    def __init__(self, is_ctx, ctx_before, lat_before, pair, slot):
        self.is_ctx, self.ctx_before, self.lat_before = is_ctx, ctx_before, lat_before
        self.index = lat_before + ctx_before
        self.pair, self.slot = pair, slot

    def following(self):
        pair = self.pair + 1 if self.slot else self.pair
        if self.is_ctx and self.ctx_before + 1 < NCTX:
            return Tile(True, self.ctx_before + 1, 0, pair, 1 - self.slot)
        return Tile(False, NCTX, self.lat_before + (0 if self.is_ctx else 1), pair, 1 - self.slot)


def projection_tile(i, slot):
    return Tile(False, NCTX, 2 * i + slot, i + NCTX // 2, slot)


def latent_tile(i, slot):
    return Tile(False, 0, 2 * i + slot, i, slot)


class Signal:

    def __init__(self, sem, lat, ctx=0, base=0):
        self.sem, self.lat, self.ctx, self.base = sem, lat, ctx, base

    def value(self, tile, k):
        return tile.lat_before * self.lat + (self.ctx * tile.ctx_before + k + self.base)

    def wait(self, eng, tile, k):
        value = self.value(tile, k)
        if not (isinstance(value, int) and value <= 0):
            eng.wait_ge(self.sem, value)

    def wait_all(self, eng, tile):
        self.wait(eng, tile, self.ctx if tile.is_ctx else self.lat)

    def wait_before(self, eng, tile):
        self.wait(eng, tile, 0)


class Chain:

    def __init__(self, eng, signal, tile):
        self.eng, self.counts, self.tile, self.n = eng, signal, tile, 0

    def __call__(self, ins):
        self.n += 1
        ins.then_inc(self.counts.sem, 1)
        self.counts.wait(self.eng, self.tile, self.n)

    def close(self):
        want = self.counts.ctx if self.tile.is_ctx else self.counts.lat
        assert self.n == want, (self.n, want)


def build(nc, A, out):
    with ExitStack() as ctx:
        def sb(name, shape, dt=F32):
            return ctx.enter_context(nc.sbuf_tensor(name, shape, dt))

        def sem(name):
            return ctx.enter_context(nc.semaphore(name))

        def scratch(name, shape, dt=F32):
            return nc.dram_tensor(name, shape, dt, kind="Internal").ap()

        pack = scratch("pack", [NTOK + 1, P, PACKW])
        mixed = scratch("mixed", [NLAT, P, D])
        resid = scratch("resid", [NLAT, P, D])
        normed = scratch("normed", [SEQ, D])
        slots_d = scratch("slots_d", [P * NBLK, 1], I32)
        expert_out = scratch("expert_out", [P * (EXPERTS + NOVER), D])

        colv = sb("colv", [P, C_END])
        rowv = sb("rowv", [P, W_END])
        consts = sb("consts_sb", [P, I_END])
        ident = consts[:, I_ID:I_ID + P]
        cact = sb("cact", [P, KD, 2])
        modc = sb("modc", [P, 48, 2])
        scale1 = sb("scale1", [P, KD, 2])
        scale2 = sb("scale2", [P, KD])
        halfs = sb("halfs", [P, 16])
        stat = sb("stat", [P, 96])
        negsink = sb("negsink", [P, 4])
        sub8 = sb("sub8", [P, 64])
        lgam = sb("lgam", [P, 8])
        neglam = sb("neglam", [P, 1])
        decay = sb("decay", [P, 4, 4])
        gl = sb("gl", [P, 4, 64])
        dmask = sb("dmask", [P, 4, P])
        g1row = sb("g1row", [P, D])
        g2row = sb("g2row", [P, D])
        ST = sb("ST", [P, NLAT, 256])
        wr = sb("wr", [P, KD, 36])
        logits = sb("logits", [P, NLAT, 36])
        onesm = sb("onesm", [P, P])
        pairw = sb("pairw", [P, 2, NLAT])
        slot_at = sb("slot_at", [P, 2, NLAT], I32)
        row_at = sb("row_at", [P, 2, NLAT], I32)
        slots = sb("slots", [P, NBLK], I32)
        idxc = sb("idxc", [P, 2], I32)
        tokid = sb("tokid", [P, NLAT], I32)
        gidx = sb("gidx", [P, 2, 2], I32)
        ctl = sb("ctl", [P, NOVER + 2], I32)

        arena_cols = 44160
        arena = sb("arena", [P, arena_cols])

        class Region:

            def __init__(self, start=0):
                self.at = start

            def __call__(self, *shape):
                n = int(np.prod(shape))
                a = arena[:, self.at:self.at + n]
                self.at += n
                assert self.at <= arena_cols, self.at
                if len(shape) == 2:
                    a = a.rearrange("p (a b) -> p a b", a=shape[0])
                if len(shape) == 3:
                    a = a.rearrange("p (a b c) -> p a b c", a=shape[0], b=shape[1])
                return a

        banks = ctx.enter_context(nc.psum_tensor("banks", [P, 8, 512], F32))
        psum = [banks[:, i] for i in range(8)]

        ones = Tile(True, 0, 0, 0, 0)
        zero_out = sem("zero_out")
        rows_in = sem("rows_in")
        consts_in = sem("consts_in")
        cols_in = sem("cols_in")
        cols_turned = sem("cols_turned")
        cols_ready = sem("cols_ready")
        cact_ready = sem("cact_ready")
        act_setup = Signal(sem("act_setup"), 0, 3)
        vec_setup = Signal(sem("vec_setup"), 0, 26)
        abs_ready = sem("abs_ready")
        lgam_ready = sem("lgam_ready")
        lam_dot = sem("lam_dot")
        lam_exp = sem("lam_exp")
        decay_exp = sem("decay_exp")
        halfs_ready = sem("halfs_ready")
        pads_ready = sem("pads_ready")
        w_up_in = sem("w_up_in")
        mod_in = [sem("mod_in0"), sem("mod_in1")]
        mod_done = sem("mod_done")
        mod_saved = sem("mod_saved")

        rb = Region()
        w_in_sb = rb(KD, DIN)
        w_uq_sb = rb(2, 384)
        w_ukv_sb = rb(512)
        xs = rb(2, D)
        tab = rb(2, T_END)
        xn = rb(D)
        hT = [rb(KD, P) for _ in range(2)]
        qm2 = rb(4, 96)
        qmr = rb(4, 32)
        qmt = rb(4, 32)
        km = rb(4, 96)
        kfb = rb(4, P)
        qfb = rb(4, P)
        lor = rb(384)
        lorT = rb(3, P)
        junk = rb(384)
        mod_at = rb.at
        z = rb(1824)
        R = rb(1824)
        rt = rb(896)
        packs = rb(PACKW)
        mod_w = [Region(mod_at)(KD, 512), Region(mod_at + KD * 512)(KD, 512)]
        colrows = Region(mod_at + 2 * KD * 512)(P)
        dexp = Region(mod_at + 2 * KD * 512 + P)(4, P)

        def mod_load(eng, bufs, group, slot):
            eng.dma_start(bufs[slot], A["w_mod"].rearrange("a (k p) (g c) -> g p (a k) c", p=P, c=512)
                          [ds(group, 1)].rearrange("a p k c -> p (a k) c")).then_inc(mod_in[slot], 16)

        def mod_matmuls(pe, bufs, slot, where):
            for j in range(4):
                for k in range(KD):
                    mm = pe.matmul(where[:, 2 * j:2 * j + 2], bufs[slot][:, k, j * P:(j + 1) * P],
                                   cact[:, k, :], start=(k == 0), stop=(k == KD - 1))
            return mm

        def mod_save(dve, group, where):
            dve.tensor_copy(modc.rearrange("p j w -> p (j w)")[:, ds(group * 8, 8)], where[:, 0:8]
                            ).then_inc(mod_saved, 1)

        def add_bias(dve, lo, hi):
            return dve.tensor_tensor(modc[:, lo:hi], modc[:, lo:hi],
                                     colv[:, C_BMOD + lo:C_BMOD + hi].unsqueeze(2).to_broadcast([P, hi - lo, 2]),
                                     ALU.add)

        MOD_FIRST = 4

        def a_sync(sp):
            sp.dma_start(colrows[0:C_END], A["cols"]).then_inc(cols_in, 16)
            for group in range(2):
                mod_load(sp, mod_w, group, group)
            sp.dma_start(pack[NTOK, :, K_S:K_S + 256], A["zeros"][:, 0:256]).then_inc(zero_out, 16)
            sp.dma_start(consts[:, :], A["consts"]).then_inc(consts_in, 16)
            sp.dma_start(rowv[:, :], A["rows"].to_broadcast([P, W_END])).then_inc(rows_in, 16)
            b_load(sp, ctx_tiles()[0])
            for n, (c, w, _) in enumerate(CHUNKS):
                if n == len(CHUNKS) // 2:
                    for group in range(2, MOD_FIRST):
                        sp.wait_ge(mod_done, group - 1)
                        mod_load(sp, mod_w, group, group % 2)
                sp.dma_start(w_in_sb[:, :, c:c + w], A["w_in"].rearrange("a (k p) c -> p (a k) c", p=P)[:, :, c:c + w]
                             ).then_inc(w_in_in[n], 16)
            sp.dma_start(w_uq_sb, A["w_uq"].rearrange("a (k p) c -> p (a k) c", p=P)).then_inc(w_up_in, 16)
            sp.dma_start(w_ukv_sb, A["w_ukv"].rearrange("a p c -> p (a c)")).then_inc(w_up_in, 16)

        def a_tensor(pe):
            pe.wait_ge(cols_in, 16)
            pe.wait_ge(consts_in, 16)
            pe.transpose(psum[5][:, 0:C_END], colrows[0:C_END], ident[0:C_END, 0:C_END]).then_inc(cols_turned, 1)
            pe.wait_ge(cact_ready, 1)
            for group in range(MOD_FIRST):
                slot = group % 2
                pe.wait_ge(mod_in[slot], 16 * (group // 2 + 1))
                if group >= 2:
                    pe.wait_ge(mod_saved, group - 1)
                mod_matmuls(pe, mod_w, slot, psum[6 + slot]).then_inc(mod_done, 1)

        def a_scalar(act):
            step = Chain(act, act_setup, ones)
            act.wait_ge(cols_ready, 1)
            act.activation(cact.rearrange("p k w -> p w k"), colv[:, 0:16].rearrange("p (w k) -> p w k", w=2),
                           ACT.Silu).then_inc(cact_ready, 1)
            act.wait_ge(abs_ready, 1)
            step(act.activation(stat[:, 24:32], stat[:, 16:24], ACT.Exp, scale=-1.0))
            step(act.activation(stat[:, 32:40], stat[:, 24:32], ACT.Copy, bias=1.0))
            step(act.activation(stat[:, 40:48], stat[:, 32:40], ACT.Ln))
            act.wait_ge(lam_dot, 1)
            act.activation(stat[:, 66:68], stat[:, 64:66], ACT.Exp).then_inc(lam_exp, 1)
            act.wait_ge(lgam_ready, 1)
            act.wait_ge(consts_in, 16)
            for kind, (direction, s) in enumerate(((0, 0), (1, 1), (0, 2), (1, 3))):
                act.activation(decay[:, kind], lgam[:, 4 * direction:4 * direction + 4], ACT.Exp,
                               scale=consts[:, I_STEP + s:I_STEP + s + 1]).then_inc(decay_exp, 1)
            for half in range(2):
                lo, hi = 64 * half, 64 * half + 64
                act.activation(gl[lo:hi], lgam[lo:hi, 4 * half:4 * half + 4].unsqueeze(2).to_broadcast([64, 4, 64]),
                               ACT.Exp, scale=float(P)).then_inc(decay_exp, 1)
            for h in range(4):
                act.activation(dmask[:, h], consts[:, I_REL:I_REL + P], ACT.Exp, scale=lgam[:, h:h + 1]
                               ).then_inc(decay_exp, 1)
                act.activation(dexp[:, h], consts[:, I_RELB:I_RELB + P], ACT.Exp, scale=lgam[:, 4 + h:5 + h]
                               ).then_inc(decay_exp, 1)

        def a_vector(dve):
            step = Chain(dve, vec_setup, ones)
            step(dve.memset(halfs[:, 0:4], -0.5))
            step(dve.memset(halfs[:, 4:5], 1.0 / 128))
            step(dve.memset(halfs[:, 6:7], 1.0 / D))
            step(dve.memset(halfs[:, 7:8], 1.0 / 64))
            step(dve.memset(halfs[:, 8:16], EPS))
            dve.memset(halfs[:, 5:6], 1.0 / 256).then_inc(halfs_ready, 1)
            dve.wait_ge(cols_turned, 1)
            dve.tensor_copy(colv[:, :], psum[5][:, 0:C_END]).then_inc(cols_ready, 1)
            dve.wait_ge(rows_in, 16)
            x = rowv[:, W_DECAY:W_DECAY + 8]
            step(dve.tensor_scalar(negsink[:, :], rowv[:, W_SINK:W_SINK + 4], -1.0, None, ALU.mult))
            step(dve.tensor_scalar(sub8[:, :], rowv[:, W_SUBLN:W_SUBLN + 64], 1.0 - LAMBDA_INIT, None, ALU.mult))
            step(dve.tensor_scalar(stat[:, 48:56], x, -1.0, None, ALU.mult))
            dve.tensor_tensor(stat[:, 16:24], x, stat[:, 48:56], ALU.max).then_inc(abs_ready, 1)
            step(dve.tensor_tensor(rowv[:, W_LAM:W_LAM + 64], rowv[:, W_LAM:W_LAM + 64],
                                   rowv[:, W_LAM + 64:W_LAM + 128], ALU.mult))
            dve.tensor_reduce(stat[:, 64:66], rowv[:, W_LAM:W_LAM + 64].rearrange("p (a b) -> p a b", a=2),
                              AX.X, ALU.add).then_inc(lam_dot, 1)
            act_setup.wait(dve, ones, 3)
            y, u, lnu, t, lg = stat[:, 24:32], stat[:, 32:40], stat[:, 40:48], stat[:, 56:64], lgam[:, :]
            step(dve.tensor_scalar(stat[:, 70:78], u, -1.0, None, ALU.add))
            step(dve.tensor_scalar(t, stat[:, 70:78], 1e-30, None, ALU.max))
            step(dve.reciprocal(stat[:, 78:86], t))
            step(dve.tensor_tensor(t, y, stat[:, 78:86], ALU.mult))
            step(dve.tensor_tensor(t, t, lnu, ALU.mult))
            step(dve.tensor_scalar(stat[:, 86:94], stat[:, 70:78], 0.0, None, ALU.is_equal))
            step(dve.tensor_tensor(stat[:, 86:94], stat[:, 86:94], y, ALU.mult))
            step(dve.tensor_tensor(t, t, stat[:, 86:94], ALU.add))
            step(dve.tensor_scalar(stat[:, 48:56], x, 0.0, None, ALU.min))
            dve.tensor_tensor(lg, stat[:, 48:56], t, ALU.subtract).then_inc(lgam_ready, 1)
            dve.wait_ge(lam_exp, 1)
            step(dve.tensor_tensor(stat[:, 94:95], stat[:, 67:68], stat[:, 66:67], ALU.subtract))
            step(dve.tensor_scalar(neglam[:, :], stat[:, 94:95], -LAMBDA_INIT, None, ALU.add))
            dve.wait_ge(decay_exp, 14)
            for m, c in ((dmask[:, :], I_MF), (dexp, I_MB)):
                step(dve.tensor_tensor(m, m,
                                       consts[:, c:c + P].unsqueeze(1).to_broadcast([P, 4, P]), ALU.mult))
            step(dve.tensor_tensor(dmask[:, :], dmask[:, :], dexp, ALU.add))
            for group in range(MOD_FIRST):
                dve.wait_ge(mod_done, group + 1)
                mod_save(dve, group, psum[6 + group % 2])
            dve.wait_ge(mod_saved, MOD_FIRST)
            step(add_bias(dve, 0, 16))
            step(dve.tensor_scalar(scale1[:, :], modc[:, 8:16], 1.0, None, ALU.add))
            step(dve.tensor_tensor(scale1[:, :], scale1[:, :],
                                   colv[:, C_N1:C_N1 + 8].unsqueeze(2).to_broadcast([P, KD, 2]), ALU.mult))
            dve.wait_ge(mod_done, MOD_FIRST)
            dve.memset(packs[96:128, :], 0.0).then_inc(pads_ready, 1)
            step.close()
            dve.wait_ge(pads_ready, 1)

        x_in = [sem("x_in0"), sem("x_in1")]
        tab_in = [sem("tab_in0"), sem("tab_in1")]
        w_in_in = [sem(f"w_in_in{n}") for n in range(len(CHUNKS))]

        def signal(name, lat, c=0, base=0):
            return Signal(sem(name), lat, c, base)

        x_sq = signal("x_sq", 1, 1)
        x_rstd = signal("x_rstd", 3, 3)
        x_norm = signal("x_norm", 1, 1)
        x_turned = signal("x_turned", 2, 2)
        h_ready = signal("h_ready", 8, 8)
        chunk_done = signal("chunk_done", 6, 5)
        chunk_saved = signal("chunk_saved", 7, 6)
        lora_sq = signal("lora_sq", 2, 1)
        lora_rstd = signal("lora_rstd", 3, 3)
        lora_norm = signal("lora_norm", 2, 1)
        lora_turned = signal("lora_turned", 1, 1)
        lora_ready = signal("lora_ready", 3, 1)
        up_done = signal("up_done", 2, 1)
        up_saved = signal("up_saved", 4, 2)
        rot_t = signal("rot_t", 10)
        rot_c = signal("rot_c", 5)
        rot = signal("rot", 5, 0, 6)
        kr_spread = signal("kr_spread", 1, 1)
        kfb_ready = signal("kfb_ready", 2, 2)
        qfb_ready = signal("qfb_ready", 2, 0, 1)
        turned = signal("turned", 6, 2)
        saved = signal("saved", 8, 2)
        upd_done = signal("upd_done", 1, 1)
        upd_saved = signal("upd_saved", 1, 1)
        pack_out = signal("pack_out", 16, 16)

        Z, X, T, M = psum[0:2], psum[2:4], psum[4:6], psum[6:8]

        def chunks(tile):
            return [(n, c, (cw if tile.is_ctx else lw)) for n, (c, lw, cw) in enumerate(CHUNKS)
                    if not tile.is_ctx or cw]

        def nth(tile, n):
            return [m for m, _, _ in chunks(tile)].index(n)

        def zbank(tile, n):
            return (5 * tile.ctx_before + nth(tile, n)) % 2

        def heads_of(t, c, heads, w):
            return t[:, c:c + heads * w].rearrange("p (h w) -> p h w", h=heads)

        def b_load(sp, tile):
            x_norm.wait(sp, tile, -1)
            sp.dma_start(xs[:, tile.slot], A["tokens"][ds(tile.index, 1)].rearrange("a p d -> p (a d)")
                         ).then_inc(x_in[tile.slot], 16)

        def b_load_tables(sp, tile):
            rot.wait(sp, tile, -5)
            sp.dma_start(tab[:, tile.slot], A["tables"][ds(tile.lat_before, 1)].rearrange("a p d -> p (a d)")
                         ).then_inc(tab_in[tile.slot], 16)

        def b_sync(sp, tile):
            b_load(sp, tile.following())
            if not tile.is_ctx:
                b_load_tables(sp, tile)
            for done in (saved, upd_saved, up_saved, chunk_saved):
                done.wait_all(sp, tile)
            w = KVW if tile.is_ctx else PACKW
            sp.dma_start(pack[ds(tile.index, 1)].rearrange("a p c -> p (a c)")[:, 0:w], packs[:, 0:w]
                         ).then_inc(pack_out.sem, 16)

        def b_prep_scalar(act, tile):
            act.wait_ge(x_in[tile.slot], 16 * (tile.pair + 1))
            x_turned.wait_before(act, tile)
            act.activation(xn, xs[:, tile.slot], ACT.Square, accum_out=stat[:, 0:1]).then_inc(x_sq.sem, 1)
            x_rstd.wait(act, tile, 3)
            act.activation(xn, xs[:, tile.slot], ACT.Copy, scale=stat[:, 2:3]).then_inc(x_norm.sem, 1)

        def b_prep_pool(pool, tile):
            x_sq.wait(pool, tile, 1)
            pool.tensor_tensor(stat[:, 3:4], stat[:, 0:1], halfs[:, 6:7], ALU.mult).then_inc(x_rstd.sem, 1)
            x_rstd.wait(pool, tile, 1)
            pool.tensor_tensor(stat[:, 1:2], stat[:, 3:4], halfs[:, 8:9], ALU.add).then_inc(x_rstd.sem, 1)
            x_rstd.wait(pool, tile, 2)
            pool.tensor_tensor(stat[:, 2:3], stat[:, 1:2], halfs[:, 0:1], ALU.pow).then_inc(x_rstd.sem, 1)

        def b_prep_tensor(pe, tile):
            x_norm.wait(pe, tile, 1)
            h_ready.wait_before(pe, tile)
            for half in range(2):
                for j in range(4):
                    k = 4 * half + j
                    mm = pe.transpose(X[half][:, j * P:(j + 1) * P], xn[:, k * P:(k + 1) * P], ident)
                mm.then_inc(x_turned.sem, 1)

        def b_prep_vector(dve, tile):
            w = 1 if tile.is_ctx else 0
            for k in range(KD):
                if k % 4 == 0:
                    x_turned.wait(dve, tile, k // 4 + 1)
                dve.tensor_scalar(hT[tile.slot][:, k], X[k // 4][:, (k % 4) * P:(k % 4 + 1) * P],
                                  scale1[:, k, w:w + 1], modc[:, k, w:w + 1], ALU.mult, ALU.add
                                  ).then_inc(h_ready.sem, 1)

        def b_tensor(pe, tile):
            def chunk(n):
                pos = nth(tile, n)
                _, c, w = chunks(tile)[pos]
                if tile.is_ctx and tile.ctx_before == 0 or tile.is_ctx is False:
                    pe.wait_ge(w_in_in[n], 16)
                chunk_saved.wait(pe, tile, pos - 1 if pos >= 2 else (-2, 0)[pos])
                for k in range(KD):
                    if pos == 0:
                        h_ready.wait(pe, tile, k + 1)
                    mm = pe.matmul(Z[zbank(tile, n)][:, 0:w], hT[tile.slot][:, k], w_in_sb[:, k, c:c + w],
                                   start=(k == 0), stop=(k == KD - 1))
                mm.then_inc(chunk_done.sem, 1)

            def turn(bank, sources, rows=P):
                for j, src in enumerate(sources):
                    mm = pe.transpose(bank[0:rows, j * P:(j + 1) * P], src, ident)
                mm.then_inc(turned.sem, 1)

            chunk(0)
            chunk(1)
            lora_norm.wait_all(pe, tile)
            saved.wait_before(pe, tile)
            for j in range(1 if tile.is_ctx else 3):
                mm = pe.transpose(T[0][:, j * P:(j + 1) * P], lor[:, j * P:(j + 1) * P], ident)
            mm.then_inc(lora_turned.sem, 1)
            if not tile.is_ctx:
                chunk(2)
            if tile.is_ctx:
                pe.wait_ge(w_up_in, 32)
            upd_saved.wait_before(pe, tile)
            up_saved.wait_before(pe, tile)
            lora_ready.wait(pe, tile, 1)
            pe.matmul(M[1][:, 0:512], lorT[:, 0], w_ukv_sb, start=True, stop=True).then_inc(up_done.sem, 1)
            if not tile.is_ctx:
                lora_ready.wait(pe, tile, 3)
                pe.matmul(M[0][:, 0:384], lorT[:, 1], w_uq_sb[:, 0], start=True, stop=False)
                pe.matmul(M[0][:, 0:384], lorT[:, 2], w_uq_sb[:, 1], start=False, stop=True).then_inc(up_done.sem, 1)
            chunk(3)
            kr_spread.wait(pe, tile, 1)
            up_saved.wait(pe, tile, 1)
            turn(T[1], [km[:, h] for h in range(4)], 96)
            b_prep_tensor(pe, tile.following())
            chunk(4)
            lora_ready.wait_all(pe, tile)
            if tile.is_ctx:
                chunk_saved.wait(pe, tile, nth(tile, 3) + 1)
                turn(T[0], [z[:, c:c + P] for c in (Z_DK, Z_DK + P, Z_SK)])
                chunk(5)
            else:
                rot.wait(pe, tile, 4)
                turn(T[0], [R[:, c:c + P] for c in (Z_DK, Z_DK + P, Z_SK)])
                saved.wait(pe, tile, 1)
                turn(T[1], [R[:, c:c + P] for c in (Z_SQ, Z_SQ + P, Z_DQ, Z_DQ + P)])
                chunk(5)
                saved.wait(pe, tile, 2)
                turn(T[0], [R[:, c:c + P] for c in (Z_RQ, Z_RQ + P, Z_RK, Z_RK + P)])
                saved.wait(pe, tile, 4)
                qfb_ready.wait_all(pe, tile)
                turn(T[1], [qfb[:, h] for h in range(4)])
                saved.wait(pe, tile, 6)
                rot.wait(pe, tile, 5)
                up_saved.wait(pe, tile, 3)
                turn(T[0], [qm2[:, h] for h in range(4)], 96)
            kfb_ready.wait_all(pe, tile)
            chunk_saved.wait(pe, tile, 6)
            up_saved.wait_all(pe, tile)
            for h in range(4):
                v = KVW + V_R + 64 * h
                mm = pe.matmul(M[0][:, h * 64:(h + 1) * 64], kfb[:, h], packs[:, v:v + 64], start=True, stop=True)
            mm.then_inc(upd_done.sem, 1)

        def b_scalar(act, tile):
            def save(n, dst, lo, hi, func=ACT.Copy):
                chunk_done.wait(act, tile, nth(tile, n) + 1)
                return act.activation(dst, Z[zbank(tile, n)][:, lo:hi], func).then_inc(chunk_saved.sem, 1)

            for done in (lora_norm, rot, turned, kfb_ready, lora_sq):
                done.wait_before(act, tile)
            w0, w3 = (160, 256) if tile.is_ctx else (416, 512)
            save(0, z[:, 0:w0], 0, w0)
            chunk_saved.wait(act, tile, 1)
            act.activation(junk[:, 0:P], z[:, Z_KVL:Z_KVL + P], ACT.Square, accum_out=stat[:, 4:5]
                           ).then_inc(lora_sq.sem, 1)
            if not tile.is_ctx:
                act.activation(junk[:, P:384], z[:, Z_QL:Z_QL + 256], ACT.Square, accum_out=stat[:, 5:6]
                               ).then_inc(lora_sq.sem, 1)
            save(1, z[:, Z_SK:Z_SQ], 0, 384)
            b_prep_scalar(act, tile.following())
            if not tile.is_ctx:
                save(2, z[:, Z_SQ:Z_DK], 0, 512)
            up_done.wait(act, tile, 1)
            act.activation(km[:, :, 0:64], M[1][:, 0:256].rearrange("p (h d) -> p h d", h=4), ACT.Copy
                           ).then_inc(up_saved.sem, 1)
            pack_out.wait_before(act, tile)
            act.wait_ge(pads_ready, 1)
            act.activation(packs[:, V_M:V_M + 256], M[1][:, 256:512], ACT.Copy).then_inc(up_saved.sem, 1)
            if not tile.is_ctx:
                up_done.wait(act, tile, 2)
                q = M[0][:, 0:384].rearrange("p (h d) -> p h d", h=4)
                act.activation(qm2[:, :, 0:64], q[:, :, 0:64], ACT.Copy).then_inc(up_saved.sem, 1)
                act.activation(qmr, q[:, :, 64:96], ACT.Copy).then_inc(up_saved.sem, 1)
            save(3, z[:, Z_DK:Z_DK + w3], 0, w3)
            save(4, packs[:, V_S:V_M], 0, 384)
            v = KVW + V_R
            if tile.is_ctx:
                save(5, packs[:, v:v + P], 0, P)
                save(5, packs[:, v + P:v + 2 * P], P, 2 * P)
            else:
                save(5, packs[:, v:v + 256], 0, 256)
                save(5, packs[:, KVW + GATE:KVW + QW], 256, 512, ACT.Silu)
            upd_done.wait(act, tile, 1)
            act.activation(packs[:, R_U:KVW], M[0][:, 0:256], ACT.Copy).then_inc(upd_saved.sem, 1)

        def rope_parts():
            return [
                (heads_of(z, Z_KR, 1, 32), heads_of(R, Z_KR, 1, 32), heads_of(rt, 0, 1, 32), 1, 8),
                (heads_of(z, Z_SK, 6, 64), heads_of(R, Z_SK, 6, 64), heads_of(rt, 0, 6, 64), 6, 16),
                (heads_of(z, Z_SQ, 8, 64), heads_of(R, Z_SQ, 8, 64), heads_of(rt, 384, 8, 64), 8, 16),
                (heads_of(z, Z_DK, 16, 32), heads_of(R, Z_DK, 16, 32), heads_of(rt, 0, 16, 32), 16, 8),
                (qmr, qm2[:, :, 64:96], qmt, 4, 8),
            ]

        def rope_source(eng, tile, n):
            if n < 4:
                chunk_saved.wait(eng, tile, n + 1)
            else:
                up_saved.wait(eng, tile, 4)

        def b_rope_pool(pool, tile, n):
            src, _, dst, heads, nf = rope_parts()[n]
            rope_source(pool, tile, n)
            rot.wait(pool, tile, (0, 1, 0, 3, 0)[n])
            a, b = (T_N64, T_S64) if nf == 16 else (T_N32, T_S32)
            for half, c in ((0, a), (1, b)):
                t = tab[:, tile.slot, c:c + 2 * nf].rearrange("p (o x f) -> p o x f", o=1, x=2
                                                              ).to_broadcast([P, heads, 2, nf])
                d, s = (v.rearrange("p h (x s f) -> p h x s f", x=2, s=2) for v in (dst, src))
                pool.tensor_tensor(d[:, :, :, half, :], s[:, :, :, 1 - half, :], t, ALU.mult
                                   ).then_inc(rot_t.sem, 1)

        def b_rope_vector(dve, tile, n):
            src, dst, tmp, heads, nf = rope_parts()[n]
            rope_source(dve, tile, n)
            c = T_C64 if nf == 16 else T_C32
            t = tab[:, tile.slot, c:c + 4 * nf].unsqueeze(1).to_broadcast([P, heads, 4 * nf])
            dve.tensor_tensor(dst, src, t, ALU.mult).then_inc(rot_c.sem, 1)
            rot_c.wait(dve, tile, n + 1)
            rot_t.wait(dve, tile, 2 * n + 2)
            dve.tensor_tensor(dst, dst, tmp, ALU.add).then_inc(rot.sem, 1)

        def decayed(pool, src, dst, kinds, done):
            for s, kind in enumerate(kinds):
                pool.tensor_tensor(dst[:, :, 64 * s:64 * s + 64], src,
                                   decay[:, kind].unsqueeze(2).to_broadcast([P, 4, 64]), ALU.mult
                                   ).then_inc(done.sem, 1)

        def b_pool(pool, tile):
            lora_sq.wait_all(pool, tile)
            lora_norm.wait_before(pool, tile)
            n = 1 if tile.is_ctx else 2
            pool.tensor_tensor(stat[:, 6:6 + n], stat[:, 4:4 + n], halfs[:, 4:4 + n], ALU.mult
                               ).then_inc(lora_rstd.sem, 1)
            lora_rstd.wait(pool, tile, 1)
            pool.tensor_tensor(stat[:, 8:8 + n], stat[:, 6:6 + n], halfs[:, 8:8 + n], ALU.add
                               ).then_inc(lora_rstd.sem, 1)
            lora_rstd.wait(pool, tile, 2)
            pool.tensor_tensor(stat[:, 10:10 + n], stat[:, 8:8 + n], halfs[:, 0:n], ALU.pow
                               ).then_inc(lora_rstd.sem, 1)
            if not tile.is_ctx:
                pool.wait_ge(tab_in[tile.slot], 16 * tile.pair)
                b_rope_pool(pool, tile, 0)
            b_prep_pool(pool, tile.following())
            if not tile.is_ctx:
                b_rope_pool(pool, tile, 1)
                rot.wait(pool, tile, 2)
            else:
                chunk_saved.wait(pool, tile, 2)
            upd_done.wait_before(pool, tile)
            decayed(pool, heads_of(z if tile.is_ctx else R, Z_RK, 4, 64), kfb, (2, 3), kfb_ready)
            if not tile.is_ctx:
                b_rope_pool(pool, tile, 2)
                rot.wait(pool, tile, 3)
                turned.wait_before(pool, tile)
                decayed(pool, heads_of(R, Z_RQ, 4, 64), qfb, (0, 1), qfb_ready)
                b_rope_pool(pool, tile, 3)
                b_rope_pool(pool, tile, 4)

        def b_vector(dve, tile):
            def save(group, dst, bank, scale=None):
                turned.wait(dve, tile, group)
                if scale is None:
                    dve.tensor_copy(dst, bank).then_inc(saved.sem, 1)
                else:
                    dve.tensor_scalar(dst, bank, scale, None, ALU.mult).then_inc(saved.sem, 1)

            def b3(c, rows=P):
                return packs[0:rows, c:c + 512]

            lora_rstd.wait(dve, tile, 3)
            lora_turned.wait_before(dve, tile)
            dve.tensor_scalar(lor[:, 0:P], z[:, Z_KVL:Z_KVL + P], stat[:, 10:11], None, ALU.mult
                              ).then_inc(lora_norm.sem, 1)
            if not tile.is_ctx:
                dve.tensor_scalar(lor[:, P:384], z[:, Z_QL:Z_QL + 256], stat[:, 11:12], None, ALU.mult
                                  ).then_inc(lora_norm.sem, 1)
                for done in (turned, kfb_ready, qfb_ready):
                    done.wait_before(dve, tile)
                dve.wait_ge(tab_in[tile.slot], 16 * tile.pair)
                b_rope_vector(dve, tile, 0)
            lora_turned.wait(dve, tile, 1)
            up_done.wait_before(dve, tile)
            gains = [colv[:, C_KVG:C_KVG + 1], colv[:, C_QG:C_QG + 1], colv[:, C_QG + 1:C_QG + 2]]
            for j in range(1 if tile.is_ctx else 3):
                dve.tensor_scalar(lorT[:, j], T[0][:, j * P:(j + 1) * P], gains[j], None, ALU.mult
                                  ).then_inc(lora_ready.sem, 1)
            turned.wait_before(dve, tile)
            if tile.is_ctx:
                chunk_saved.wait(dve, tile, 1)
            else:
                rot.wait(dve, tile, 1)
            kr = (z if tile.is_ctx else R)[:, Z_KR:Z_KR + 32]
            dve.tensor_copy(km[:, :, 64:96], kr.unsqueeze(1).to_broadcast([P, 4, 32])).then_inc(kr_spread.sem, 1)
            if not tile.is_ctx:
                b_rope_vector(dve, tile, 1)
                b_rope_vector(dve, tile, 2)
            pack_out.wait_before(dve, tile)
            save(1, packs[0:96, K_M:K_M + 512], T[1][0:96, :])
            chunk_done.wait_before(dve, tile)
            b_prep_vector(dve, tile.following())
            if tile.is_ctx:
                save(2, packs[:, K_D:K_D + 384], T[0][:, 0:384])
                return
            b_rope_vector(dve, tile, 3)
            save(2, packs[:, K_D:K_D + 384], T[0][:, 0:384])
            b_rope_vector(dve, tile, 4)
            save(3, packs[:, KVW + Q_S:KVW + Q_S + 256], T[1][:, 0:256], 0.125)
            save(3, packs[:, KVW + Q_D:KVW + Q_D + 256], T[1][:, 256:512], 32.0 ** -0.5)
            save(4, packs[:, KVW + Q_R:KVW + Q_R + 256], T[0][:, 0:256], 0.125)
            save(4, packs[:, KVW + K_R:KVW + K_R + 256], T[0][:, 256:512])
            save(5, packs[:, KVW + Q_FB:KVW + Q_FB + 512], T[1][:, :], 0.125)
            save(6, packs[0:96, KVW + Q_M:KVW + Q_M + 512], T[0][0:96, :], 96.0 ** -0.5)

        def ctx_tiles():
            return [Tile(True, n, 0, n // 2, n % 2) for n in range(NCTX)]

        NV = 12
        BEFORE = {8: 10, 9: 12, 10: 14, 11: 16}
        BETWEEN = {v: v + 2 for v in range(8)} | {8: 11, 9: 13, 10: 15, 11: 17}
        BLOCKS = [5] * 4 + [10] * 8
        GROUPS = [[(lo, min(lo + 4, n)) for lo in range(0, n, 4)] for n in BLOCKS]

        def group_no(v, g):
            return sum(len(x) for x in GROUPS[:v]) + g

        def item_no(v, g):
            return sum(len(x) + 1 for x in GROUPS[:v]) + g

        def item_bank(v, g):
            return psum[6 + item_no(v, g) % 2]

        NGROUP = group_no(NV, 0)

        rd = Region()
        KV = rd(NTOK, KVW)
        qp = rd(2, QW)
        win = [rd(3, 256) for _ in range(2)]
        maskt = rd(2, 256)
        probs = rd(3, 1280)
        probsT = rd(2, 1280)
        aT = rd(4, P)
        yraw = rd(NV, 64)
        tmpd = rd(8, 64)
        tmpe = rd(8, 64)
        gg = rd(256)
        y = rd(D)
        dstat = rd(96)
        modrow = rd(512)
        w_out_at = arena_cols - KD * D
        mod_w2 = [Region(w_out_at)(KD, 512), Region(w_out_at + KD * 512)(KD, 512)]
        stmp = tmpe[:, 0:4]
        shift = dstat[:, 0:16]
        total = dstat[:, 16:32]
        raws = dstat[:, 32:36]
        ratio = dstat[:, 36:44]
        sinks = dstat[:, 44:48]
        sinke = dstat[:, 48:52]
        rtotal = dstat[:, 52:68]
        rsum, rmean = dstat[:, 68:72], dstat[:, 72:76]
        ss8, rr8 = dstat[:, 76:84], dstat[:, 84:92]
        msd = rd(16)
        assert rd.at <= w_out_at

        kv_in = [sem(f"kv_in{n}") for n in range(3)]
        q_in = [sem("q_in0"), sem("q_in1")]
        spare_out = sem("spare_out")
        pe_go = sem("pe_go")
        modrow_saved = sem("modrow_saved")
        fwd_state = sem("fwd_state")
        bwd_state = sem("bwd_state")
        s_done = signal("s_done", 18)
        masked = signal("masked", 8)
        maxed = signal("maxed", 16)
        exped = signal("exped", 16)
        ratios = signal("ratios", 8)
        combined = signal("combined", 4)
        t_done = signal("t_done", NGROUP, 0, 1)
        pt_act = signal("pt_act", 20, 0, 1)
        pt_dve = signal("pt_dve", 12, 0, 1)
        av_done = signal("av_done", NV, 0, 2)
        o_saved = signal("o_saved", NV, 0, 1)
        a_ready = signal("a_ready", 1, 0, 1)
        ret_saved = signal("ret_saved", 1, 0, 1)
        sink_sum = signal("sink_sum", 1)
        sink_exp = signal("sink_exp", 1)
        fin = signal("fin", 8, 0, 1)
        squares = signal("squares", 1)
        head_rstd = signal("head_rstd", 3)
        gated = signal("gated", 1)
        y_ready = signal("y_ready", 4, 0, 4)
        y_out = signal("y_out", 16, 0, 16)

        def d_load(sp, tile):
            t, s = tile.lat_before, tile.slot
            sp.dma_start(qp[:, s], pack[ds(t + NCTX, 1)].rearrange("a p c -> p (a c)")[:, KVW:]).then_inc(q_in[s], 16)
            sp.dma_start(win[s], pack[ds(t + NCTX - 1, 3)].rearrange("a p c -> p a c")[:, :, K_S:K_S + 256]
                         ).then_inc(q_in[s], 16)
            sp.dma_start(maskt[:, s], A["mask"][ds(t, 1)].rearrange("a p c -> p (a c)")).then_inc(q_in[s], 16)
            mod_load(sp, mod_w2, t + MOD_FIRST, s)

        def d_store(sp, tile):
            y_ready.wait_all(sp, tile)
            sp.dma_start(mixed[ds(tile.lat_before, 1)].rearrange("a p c -> p (a c)"), y).then_inc(y_out.sem, 16)

        def d_sync(sp):
            sp.wait_ge(pack_out.sem, 16 * NTOK)
            sp.wait_ge(h_ready.sem, 8 * (NTOK + 1))
            sp.wait_ge(zero_out, 16)
            for n, (lo, hi) in enumerate(((0, 2), (2, 6), (6, NTOK))):
                sp.dma_start(KV[:, lo:hi], pack[lo:hi].rearrange("a p c -> p a c")[:, :, 0:KVW]).then_inc(kv_in[n], 16)
                if n == 0:
                    d_load(sp, latent_tile(0, 0))
            d_load(sp, latent_tile(0, 1))
            sp.dma_start(expert_out[P * EXPERTS:].rearrange("(b p) c -> p b c", p=P),
                         A["zeros"].unsqueeze(1).to_broadcast([P, NOVER, D])).then_inc(spare_out, 16)
            with sp.Fori(0, NLAT // 2 - 1) as i:
                for slot in range(2):
                    d_store(sp, latent_tile(i, slot))
                    d_load(sp, latent_tile(i + 1, slot))
            for slot in range(2):
                sp.wait_ge(mod_done, MOD_GROUPS - 1 + slot)
                half = slice(KD // 2 * slot, KD // 2 * (slot + 1))
                sp.dma_start(w_out_sb[:, half], A["w_out"].rearrange("a (k p) c -> p (a k) c", p=P)[:, half]
                             ).then_inc(e_weights_in, 16)
                d_store(sp, latent_tile(NLAT // 2 - 1, slot))

        def scan_states(eng, lo, hi, first, tiles, done):
            glv = gl[lo:hi]
            n = 0

            def step(ins):
                nonlocal n
                n += 1
                ins.then_inc(done, 1)
                eng.wait_ge(done, n)

            def update(t):
                return KV[lo:hi, t, R_U:R_U + 256].rearrange("p (h e) -> p h e", h=4)

            def state(t):
                return ST[lo:hi, t].rearrange("p (h e) -> p h e", h=4)

            step(eng.tensor_tensor(stmp[lo:hi], update(first[0]), glv, ALU.mult))
            step(eng.tensor_tensor(state(tiles[0]), stmp[lo:hi], update(first[1]), ALU.add))
            for a, b in zip(tiles, tiles[1:]):
                step(eng.tensor_tensor(stmp[lo:hi], state(a), glv, ALU.mult))
                step(eng.tensor_tensor(state(b), stmp[lo:hi], update(a + NCTX), ALU.add))

        def d_tensor(pe, tile):
            t, s = tile.lat_before, tile.slot
            pe.wait_ge(q_in[s], 48 * (tile.pair + 1))

            def scores(u):
                buf = 3 * (u % 2)
                if u == 0:
                    a_ready.wait_before(pe, tile)
                elif u == 1:
                    ret_saved.wait_before(pe, tile)
                else:
                    exped.wait(pe, tile, u - 1)
                if u < 4:
                    g, r = u // 2, u % 2
                    rows = slice(64 * g, 64 * g + 64)
                    q = qp[rows, s, Q_S + P * r:Q_S + P * (r + 1)]
                    pe.matmul(psum[buf][:, 0:384], q, win[s][rows, :, 0:P], start=True, stop=True)
                    pe.matmul(psum[buf][:, 384:512], q, KV[rows, 0, K_S:K_S + P], start=True, stop=True)
                    mm = pe.matmul(psum[buf + 1][:, 0:P], q, KV[rows, 1, K_S:K_S + P], start=True, stop=True)
                elif u < 16:
                    if u == 4:
                        pe.wait_ge(kv_in[1], 16)
                        pe.wait_ge(kv_in[2], 16)
                    if u < 8:
                        rows, qc, kc = slice(0, 96), Q_M + P * (u - 4), K_M + P * (u - 4)
                    else:
                        m = u - 8
                        rows = slice(32 * (m % 4), 32 * (m % 4) + 32)
                        qc, kc = Q_D + P * (m // 4), K_D + P * (m // 4)
                    for b, (lo, hi) in enumerate(((0, 4), (4, 8), (8, 10))):
                        mm = pe.matmul(psum[buf + b][:, 0:P * (hi - lo)], qp[rows, s, qc:qc + P],
                                       KV[rows, lo:hi, kc:kc + P], start=True, stop=True)
                elif u == 16:
                    for h in range(4):
                        rows, c = slice(64 * (h % 2), 64 * (h % 2) + 64), P * (h // 2)
                        mm = pe.matmul(psum[buf + h % 2][:, c:c + P], qp[rows, s, K_R + c:K_R + c + P],
                                       qp[rows, s, Q_R + c:Q_R + c + P], start=True, stop=True)
                else:
                    if u == 17:
                        pe.wait_ge(fwd_state, 16)
                        pe.wait_ge(bwd_state, 16)
                    a_ready.wait_all(pe, tile)
                    for h in range(4):
                        where = psum[buf][:, 64 * h:64 * h + 64]
                        pe.matmul(where, aT[:, h], qp[:, s, V_R + 64 * h:V_R + 64 * h + 64], start=True, stop=False)
                        mm = pe.matmul(where, qp[:, s, Q_FB + P * h:Q_FB + P * (h + 1)],
                                       ST[:, ds(t, 1), 64 * h:64 * h + 64].rearrange("p a e -> p (a e)"),
                                       start=False, stop=True)
                mm.then_inc(s_done.sem, 1)

            def turn(v, g):
                lo, hi = GROUPS[v][g]
                if g == 0:
                    if v < 8:
                        exped.wait(pe, tile, v + 1)
                    else:
                        combined.wait(pe, tile, v - 7)
                wait_item_saved(pe, tile, item_no(v, g) - 2)
                bank = item_bank(v, g)
                src = probs[:, prob_slot(v)]
                for b in range(lo, hi):
                    mm = pe.transpose(bank[:, P * (b - lo):P * (b - lo + 1)], src[:, P * b:P * (b + 1)], ident)
                mm.then_inc(t_done.sem, 1)

            def values(v, b):
                if v < 4:
                    c = 64 * (v // 2)
                    return win[s][:, b, P + c:P + c + 64] if b < 3 else KV[:, b - 3, V_S + c:V_S + c + 64]
                c = V_M + 64 * (v - 4) if v < 8 else V_D + 64 * (v - 8)
                return KV[:, b, c:c + 64]

            def weigh(v, g):
                if g == 0:
                    wait_item_saved(pe, tile, item_no(v, len(GROUPS[v])) - 2)
                wait_item_saved(pe, tile, item_no(v, g))
                for b in range(*GROUPS[v][g]):
                    mm = pe.matmul(item_bank(v, len(GROUPS[v]))[:, 0:64], probsT[:, v % 2, P * b:P * (b + 1)], values(v, b),
                                   start=(b == 0), stop=(b == BLOCKS[v] - 1))
                if g == len(GROUPS[v]) - 1:
                    if v == MOD_UNIT:
                        pe.wait_ge(mod_saved, t + MOD_FIRST)
                        pe.sem_inc(pe_go, 1)
                        for j in range(4):
                            mm = pe.transpose(mod_place[:, 2 * j:2 * j + 2], modrow[0:2, P * j:P * (j + 1)],
                                              ident[0:2, 0:2])
                    mm.then_inc(av_done.sem, 1)

            scores(0)
            scores(1)
            pe.wait_ge(mod_in[s], 16 * (MOD_FIRST // 2) + 16 * (tile.pair + 1))
            o_saved.wait_before(pe, tile)
            for k in range(KD):
                mm = pe.matmul(psum[7][0:2], cact[:, k, :], mod_w2[s][:, k], start=(k == 0), stop=(k == KD - 1))
            mm.then_inc(mod_done, 1)
            for v in range(NV):
                if v in BEFORE:
                    scores(BEFORE[v])
                turn(v, 0)
                if v == 0:
                    pe.wait_ge(modrow_saved, t + 1)
                turn(v, 1)
                scores(BETWEEN[v])
                weigh(v, 0)
                if len(GROUPS[v]) > 2:
                    turn(v, 2)
                for g in range(1, len(GROUPS[v])):
                    weigh(v, g)

        MOD_UNIT = 5
        mod_place = item_bank(MOD_UNIT, len(GROUPS[MOD_UNIT]))[:, 64:72]

        def prob_slot(v):
            return (v if v < 8 else 8 + 2 * (v - 8)) % 3

        def wait_item_saved(eng, tile, no):
            if no < 0:
                (o_saved if no == -1 else pt_dve).wait_before(eng, tile)
                return
            v = max(u for u in range(NV) if item_no(u, 0) <= no)
            g = no - item_no(v, 0)
            if g == len(GROUPS[v]):
                o_saved.wait(eng, tile, v + 1)
            elif g == len(GROUPS[v]) - 1:
                pt_dve.wait(eng, tile, v + 1)
            else:
                pt_act.wait(eng, tile, sum(len(x) - 1 for x in GROUPS[:v]) + g + 1)

        def save_group(eng, copy, done, tile, v, g):
            lo, hi = GROUPS[v][g]
            t_done.wait(eng, tile, group_no(v, g) + 1)
            av_done.wait(eng, tile, v - 1)
            copy(probsT[:, v % 2, P * lo:P * hi], item_bank(v, g)[:, 0:P * (hi - lo)]
                 ).then_inc(done.sem, 1)

        def d_scalar(act, tile):
            def exp(u):
                if u >= 16:
                    return
                n = 640 if u < 4 else 1280
                maxed.wait(act, tile, u + 1)
                if u < 3:
                    t_done.wait_before(act, tile)
                elif u - 3 < 8:
                    t_done.wait(act, tile, group_no(u - 2, 0))
                elif (u - 3) % 2:
                    combined.wait(act, tile, (u - 3 - 8) // 2 + 1)
                else:
                    t_done.wait(act, tile, group_no(8 + (u - 3 - 8) // 2 + 1, 0))
                act.activation(probs[:, u % 3, 0:n], scores_of(u, n), ACT.Exp, bias=shift[:, u:u + 1],
                               accum_out=total[:, u:u + 1]).then_inc(exped.sem, 1)

            copy = lambda dst, src: act.activation(dst, src, ACT.Copy)
            fin.wait_before(act, tile)
            exp(0)
            exp(1)
            for v in range(NV):
                if v in BEFORE:
                    exp(BEFORE[v])
                for g in range(len(GROUPS[v]) - 1):
                    save_group(act, copy, pt_act, tile, v, g)
                exp(BETWEEN[v])
                if v == 6:
                    sink_sum.wait(act, tile, 1)
                    act.activation(sinke, sinks, ACT.Exp).then_inc(sink_exp.sem, 1)

        def scores_of(u, n):
            return banks[:, 3 * (u % 2):3 * (u % 2) + 3].rearrange("p b c -> p (b c)")[:, 0:n]

        def d_vector(dve, tile):
            s = tile.slot

            def row_max(u):
                s_done.wait(dve, tile, u + 1)
                if u == 16:
                    by_bank = [m.rearrange("p (c b) q -> p b c q", b=2) for m in (aT, dmask[:, :])]
                    dve.tensor_tensor(by_bank[0], banks[:, 0:2, 0:256].rearrange("p b (c q) -> p b c q", c=2),
                                      by_bank[1], ALU.mult).then_inc(a_ready.sem, 1)
                if u >= 16:
                    return
                n = 640 if u < 4 else 1280
                if u >= 4:
                    dve.tensor_reduce(shift[:, u:u + 1], scores_of(u, n), AX.X, ALU.max, negate=True
                                      ).then_inc(maxed.sem, 1)
                    return
                edge = psum[3 * (u % 2)].rearrange("p (b c) -> p b c", b=4)[:, 0:3:2]
                dve.tensor_tensor(edge, edge, maskt[:, s].rearrange("p (b c) -> p b c", b=2), ALU.add
                                  ).then_inc(masked.sem, 1)
                masked.wait(dve, tile, 2 * u + 1)
                dve.tensor_reduce(raws[:, u:u + 1], scores_of(u, n), AX.X, ALU.max, negate=True
                                  ).then_inc(masked.sem, 1)
                masked.wait(dve, tile, 2 * u + 2)
                dve.tensor_tensor(shift[:, u:u + 1], raws[:, u:u + 1], negsink[:, u:u + 1], ALU.min
                                  ).then_inc(maxed.sem, 1)

            def combine(h):
                u = 8 + 2 * h
                exped.wait(dve, tile, u + 2)
                dve.reciprocal(ratio[:, 2 * h:2 * h + 1], total[:, u + 1:u + 2]).then_inc(ratios.sem, 1)
                ratios.wait(dve, tile, 2 * h + 1)
                dve.scalar_tensor_tensor(ratio[:, 2 * h + 1:2 * h + 2], ratio[:, 2 * h:2 * h + 1], neglam[:, :],
                                         total[:, u:u + 1], ALU.mult, ALU.mult).then_inc(ratios.sem, 1)
                ratios.wait(dve, tile, 2 * h + 2)
                p0, p1 = probs[:, u % 3], probs[:, (u + 1) % 3]
                dve.scalar_tensor_tensor(p0, p1, ratio[:, 2 * h + 1:2 * h + 2], p0, ALU.mult, ALU.add
                                         ).then_inc(combined.sem, 1)

            def save_out(v):
                av_done.wait(dve, tile, v + 1)
                dve.tensor_copy(yraw[:, v], item_bank(v, len(GROUPS[v]))[:, 0:64]).then_inc(o_saved.sem, 1)

            fin.wait_before(dve, tile)
            y_ready.wait_before(dve, tile)
            dve.wait_ge(q_in[s], 48 * (tile.pair + 1))
            row_max(0)
            row_max(1)
            dve.wait_ge(mod_done, tile.lat_before + (MOD_FIRST + 1))
            dve.tensor_copy(modrow[0:2], psum[7][0:2]).then_inc(modrow_saved, 1)
            for v in range(NV):
                if v == MOD_UNIT + 1:
                    av_done.wait(dve, tile, v)
                    mod_save(dve, tile.lat_before + MOD_FIRST, mod_place)
                if v:
                    save_out(v - 1)
                if v in BEFORE:
                    combine(v - 8)
                    row_max(BEFORE[v])
                if v < 4:
                    save_group(dve, dve.tensor_copy, pt_dve, tile, v, len(GROUPS[v]) - 1)
                row_max(BETWEEN[v])
                if v >= 4:
                    save_group(dve, dve.tensor_copy, pt_dve, tile, v, len(GROUPS[v]) - 1)
                if v == 5:
                    maxed.wait(dve, tile, 4)
                    dve.tensor_tensor(sinks, rowv[:, W_SINK:W_SINK + 4], shift[:, 0:4], ALU.add
                                      ).then_inc(sink_sum.sem, 1)

            o4 = psum[3][:, 0:256].rearrange("p (h e) -> p h e", h=4)
            step = Chain(dve, fin, tile)
            s_done.wait(dve, tile, 18)
            step(dve.tensor_reduce(rsum, o4, AX.X, ALU.add))
            step(dve.tensor_scalar(rmean, rsum, 1.0 / 64, None, ALU.mult))
            dve.tensor_tensor(tmpd[:, 4:8], o4, rmean.unsqueeze(2).to_broadcast([P, 4, 64]), ALU.subtract
                              ).then_inc(ret_saved.sem, 1)
            ret_saved.wait_all(dve, tile)
            step(dve.tensor_tensor(tmpe[:, 4:8], tmpd[:, 4:8], tmpd[:, 4:8], ALU.mult))
            save_out(NV - 1)
            sink_exp.wait(dve, tile, 1)
            step(dve.tensor_tensor(total[:, 0:4], total[:, 0:4], sinke, ALU.add))
            step(dve.reciprocal(rtotal, total))
            o_saved.wait_all(dve, tile)
            rd_ = rtotal.rearrange("p (h m) -> p h m", m=2)
            step(dve.tensor_tensor(tmpd[:, 0:4], yraw[:, 8:12], rd_[:, 4:8, 0:1].to_broadcast([P, 4, 64]), ALU.mult))
            step(dve.tensor_tensor(tmpe[:, 0:4], tmpd[:, 0:4], tmpd[:, 0:4], ALU.mult))
            dve.tensor_reduce(ss8, tmpe, AX.X, ALU.add).then_inc(squares.sem, 1)
            y_out.wait_before(dve, tile)

            def rows(c):
                return y[:, c:c + 256].rearrange("p (h e) -> p h e", h=4)

            for c, v in ((0, 0), (768, 4)):
                dve.tensor_tensor(rows(c), yraw[:, v:v + 4], rtotal[:, v:v + 4].unsqueeze(2).to_broadcast([P, 4, 64]),
                                  ALU.mult).then_inc(y_ready.sem, 1)
            head_rstd.wait(dve, tile, 3)
            step(dve.tensor_tensor(tmpd, tmpd, rr8.unsqueeze(2).to_broadcast([P, 8, 64]), ALU.mult))
            dve.tensor_tensor(rows(256), tmpd[:, 0:4], sub8[:, :].unsqueeze(1).to_broadcast([P, 4, 64]), ALU.mult
                              ).then_inc(y_ready.sem, 1)
            gated.wait(dve, tile, 1)
            dve.tensor_tensor(rows(512), tmpd[:, 4:8], gg.rearrange("p (h e) -> p h e", h=4), ALU.mult
                              ).then_inc(y_ready.sem, 1)
            step.close()

        def d_pool(pool, tile):
            pool.wait_ge(q_in[tile.slot], 48 * (tile.pair + 1))
            y_ready.wait_before(pool, tile)
            pool.tensor_tensor(gg, qp[:, tile.slot, GATE:GATE + 256], rowv[:, W_GN:W_GN + 256], ALU.mult
                               ).then_inc(gated.sem, 1)
            squares.wait(pool, tile, 1)
            pool.tensor_tensor(msd[:, 0:8], ss8, halfs[:, 7:8].to_broadcast([P, 8]), ALU.mult
                               ).then_inc(head_rstd.sem, 1)
            head_rstd.wait(pool, tile, 1)
            pool.tensor_tensor(msd[:, 8:16], msd[:, 0:8], halfs[:, 8:16], ALU.add).then_inc(head_rstd.sem, 1)
            head_rstd.wait(pool, tile, 2)
            pool.tensor_tensor(rr8, msd[:, 8:16], halfs[:, 0:1].to_broadcast([P, 8]), ALU.pow
                               ).then_inc(head_rstd.sem, 1)

        re_ = Region()
        w_out_sb = Region(w_out_at)(KD, D)
        yin = re_(2, D)
        xin = re_(2, D)
        yT = [re_(KD, P) for _ in range(2)]
        x1 = re_(2, D)
        x1g = re_(D)
        xn2 = re_(D)
        h2T = re_(KD, P)
        estat = re_(16)
        expert_at = re_.at
        moe_w = Region(expert_at)
        wg = [None, None]
        wu = [None, None]
        wd = [None, None]
        for slot in range(2):
            wg[slot], wu[slot], wd[slot] = moe_w(KD, HIDDEN), moe_w(KD, HIDDEN), moe_w(HB, D)
        assert moe_w.at <= w_out_at

        e_weights_in = sem("e_weights_in")
        e_setup = Signal(sem("e_setup"), 0, 4)
        grow_done = sem("grow_done")
        grow_saved = sem("grow_saved")
        e_in = [sem("e_in0"), sem("e_in1")]
        y_turned = signal("y_turned", 2)
        yT_saved = signal("yT_saved", 2)
        proj_done = signal("proj_done", 2)
        gated_out = signal("gated_out", 2)
        x1_ready = signal("x1_ready", 2)
        e_sq = signal("e_sq", 1)
        e_rstd = signal("e_rstd", 3)
        n2_ready = signal("n2_ready", 1, 0, 1)
        n2_turned = signal("n2_turned", 2, 0, 1)
        h2_ready = signal("h2_ready", 8, 0, 1)
        routed = signal("routed", 1, 0, 1)
        logits_saved = signal("logits_saved", 1, 0, 1)
        x1_out = [sem("x1_out0"), sem("x1_out1")]
        n2_out = sem("n2_out")
        moe_in = [[sem(f"moe_in_{n}{s}") for n in ("gate", "up", "down")] for s in range(2)]

        def e_tile(t):
            return Tile(False, 0, t, t // 2, t % 2)

        def e_skewed(i, s):
            return Tile(False, 0, 2 * i + (1 + s), i + s, 1 - s)

        def shifted(tile, by):
            slot = 1 - tile.slot
            pair = tile.pair - (1 if by < 0 and slot else 0) + (1 if by > 0 and not slot else 0)
            return Tile(False, 0, tile.lat_before + by, pair, slot)

        def skewed(eng, body):
            body(eng, e_tile(0), True, False)
            with eng.Fori(0, NLAT // 2 - 1) as i:
                for s in range(2):
                    body(eng, e_skewed(i, s), False, False)
            body(eng, e_tile(NLAT - 1), False, True)

        def moe_load(eng, expert, slot, wait_used=None):
            for n, (dst, src) in enumerate(((wg, "w_gate"), (wu, "w_up"), (wd, "w_down"))):
                if wait_used:
                    wait_used(n)
                eng.dma_start(dst[slot], A[src][ds(expert, 1)].rearrange("a (k p) c -> p (a k) c", p=P)
                              ).then_inc(moe_in[slot][n], 16)

        def e_load(sp, tile):
            s = tile.slot
            sp.dma_start(yin[:, s], mixed[ds(tile.lat_before, 1)].rearrange("a p c -> p (a c)")).then_inc(e_in[s], 16)
            sp.dma_start(xin[:, s], A["tokens"][ds(tile.lat_before + NCTX, 1)].rearrange("a p c -> p (a c)")
                         ).then_inc(e_in[s], 16)

        def e_store(sp, tile, load_next):
            x1_ready.wait_all(sp, tile)
            sp.dma_start(resid[ds(tile.lat_before, 1)].rearrange("a p c -> p (a c)"), x1[:, tile.slot]
                         ).then_inc(x1_out[tile.slot], 16)
            if load_next:
                e_load(sp, load_next)
            n2_ready.wait_all(sp, tile)
            sp.dma_start(normed.rearrange("(t p) c -> t p c", p=P)[ds(tile.lat_before, 1)]
                         .rearrange("a p c -> p (a c)"), xn2).then_inc(n2_out, 16)

        def e_sync(sp):
            sp.wait_ge(y_out.sem, 16 * (NLAT + 1))
            for slot in range(2):
                e_load(sp, e_tile(slot))
            sp.dma_start(wr[:, :, :], A["w_route"].rearrange("(k p) c -> p k c", p=P)).then_inc(e_weights_in, 16)
            sp.dma_start(slots_d.rearrange("(p b) a -> p (b a)", p=P), A["ids"][:, NLAT:]).then_inc(ids_in, 16)
            sp.dma_start(tokid[:, :], A["ids"][:, 0:NLAT]).then_inc(ids_in, 16)
            with sp.Fori(0, NLAT // 2 - 1) as i:
                for slot in range(2):
                    e_store(sp, latent_tile(i, slot), latent_tile(i + 1, slot))
            for slot in range(2):
                e_store(sp, latent_tile(NLAT // 2 - 1, slot), None)

        def e_rows_tensor(pe):
            pe.wait_ge(e_setup.sem, 1)
            for n, base in enumerate((16, 40)):
                for half in range(2):
                    for j in range(4):
                        k = 4 * half + j
                        mm = pe.matmul(psum[2 * n + half][:, P * j:P * (j + 1)],
                                       modc[:, base + k, 0:1].to_broadcast([P, P]), ident, start=True, stop=True)
                    mm.then_inc(grow_done, 1)
            pe.wait_ge(grow_saved, 4)
            pe.wait_ge(e_weights_in, 48)

        def e_rows_vector(dve):
            dve.wait_ge(mod_saved, MOD_GROUPS)
            step = Chain(dve, e_setup, ones)
            step(add_bias(dve, 16, 48))
            step(dve.tensor_scalar(scale2[:, :], modc[:, 32:40, 0], 1.0, None, ALU.add))
            step(dve.tensor_tensor(scale2[:, :], scale2[:, :], colv[:, C_N2:C_N2 + 8], ALU.mult))
            for n, row in enumerate((g1row, g2row)):
                for half in range(2):
                    dve.wait_ge(grow_done, 2 * n + half + 1)
                    dve.tensor_copy(row[:, 512 * half:512 * (half + 1)], psum[2 * n + half]).then_inc(grow_saved, 1)
            dve.wait_ge(grow_saved, 4)
            step(dve.memset(onesm[:, :], 1.0))
            step.close()

        def e_turn(pe, tile):
            pe.wait_ge(e_in[tile.slot], 32 * (tile.pair + 1))
            yT_saved.wait_before(pe, tile)
            for half in range(2):
                for j in range(4):
                    k = 4 * half + j
                    mm = pe.transpose(psum[2 + half][:, P * j:P * (j + 1)], yin[:, tile.slot, P * k:P * (k + 1)], ident)
                mm.then_inc(y_turned.sem, 1)

        def e_project(pe, tile, half):
            gated_out.wait(pe, tile, half - 1)
            yT_saved.wait_all(pe, tile)
            for k in range(KD):
                mm = pe.matmul(psum[half], yT[tile.slot][:, k], w_out_sb[:, k, 512 * half:512 * half + 512],
                               start=(k == 0), stop=(k == KD - 1))
            mm.then_inc(proj_done.sem, 1)

        def e_turn_normed(pe, tile):
            n2_ready.wait_all(pe, tile)
            h2_ready.wait_before(pe, tile)
            for half in range(2):
                for j in range(4):
                    k = 4 * half + j
                    mm = pe.transpose(psum[4 + half][:, P * j:P * (j + 1)], xn2[:, P * k:P * (k + 1)], ident)
                mm.then_inc(n2_turned.sem, 1)

        def e_route(pe, tile):
            logits_saved.wait_before(pe, tile)
            for k in range(KD):
                h2_ready.wait(pe, tile, k + 1)
                mm = pe.matmul(psum[6][:, 0:36], h2T[:, k], wr[:, k], start=(k == 0), stop=(k == KD - 1))
            mm.then_inc(routed.sem, 1)

        def e_tensor(pe, tile, first, last):
            if first:
                e_turn(pe, tile)
            e_project(pe, tile, 0)
            if not last:
                e_turn(pe, shifted(tile, 1))
            if not first:
                e_turn_normed(pe, shifted(tile, -1))
            e_project(pe, tile, 1)
            if not first:
                e_route(pe, shifted(tile, -1))
            if last:
                e_turn_normed(pe, tile)
                e_route(pe, tile)

        def e_scalar(act, tile):
            x1_ready.wait_all(act, tile)
            n2_turned.wait_before(act, tile)
            wait_n2_out(act, tile)
            act.activation(xn2, x1[:, tile.slot], ACT.Square, accum_out=estat[:, 0:1]).then_inc(e_sq.sem, 1)
            e_rstd.wait(act, tile, 3)
            act.activation(xn2, x1[:, tile.slot], ACT.Copy, scale=estat[:, 3:4]).then_inc(n2_ready.sem, 1)

        def wait_n2_out(eng, tile):
            eng.wait_ge(n2_out, 16 * tile.lat_before + 16)

        def rstd_pool(pool, tile, st, sq, rstd):
            sq.wait(pool, tile, 1)
            pool.tensor_tensor(st[:, 1:2], st[:, 0:1], halfs[:, 6:7], ALU.mult).then_inc(rstd.sem, 1)
            rstd.wait(pool, tile, 1)
            pool.tensor_tensor(st[:, 2:3], st[:, 1:2], halfs[:, 8:9], ALU.add).then_inc(rstd.sem, 1)
            rstd.wait(pool, tile, 2)
            pool.tensor_tensor(st[:, 3:4], st[:, 2:3], halfs[:, 0:1], ALU.pow).then_inc(rstd.sem, 1)

        def e_pool(pool, tile):
            rstd_pool(pool, tile, estat, e_sq, e_rstd)

        def e_save_y(dve, tile):
            for half in range(2):
                y_turned.wait(dve, tile, half + 1)
                proj_done.wait(dve, tile, -2)
                dve.tensor_copy(yT[tile.slot][:, 4 * half:4 * half + 4],
                                psum[2 + half].rearrange("p (j q) -> p j q", j=4)).then_inc(yT_saved.sem, 1)

        def e_residual(dve, tile, half):
            s = tile.slot
            c = slice(512 * half, 512 * half + 512)
            proj_done.wait(dve, tile, half + 1)
            x1_ready.wait(dve, tile, half - 1)
            dve.tensor_tensor(x1g[:, c], psum[half], g1row[:, c], ALU.mult).then_inc(gated_out.sem, 1)
            gated_out.wait(dve, tile, half + 1)
            dve.wait_ge(x1_out[s], 16 * (tile.pair + 1))
            n2_ready.wait(dve, tile, -1)
            dve.tensor_tensor(x1[:, s, c], x1g[:, c], xin[:, s, c], ALU.add).then_inc(x1_ready.sem, 1)

        def e_modulate(dve, tile):
            routed.wait_before(dve, tile)
            for k in range(KD):
                if k % 4 == 0:
                    n2_turned.wait(dve, tile, k // 4 + 1)
                dve.tensor_scalar(h2T[:, k], psum[4 + k // 4][:, (k % 4) * P:(k % 4 + 1) * P],
                                  scale2[:, k:k + 1], modc[:, 24 + k, 0:1], ALU.mult, ALU.add
                                  ).then_inc(h2_ready.sem, 1)

        def e_save_logits(dve, tile):
            routed.wait(dve, tile, 1)
            dve.tensor_tensor(logits[:, ds(tile.lat_before, 1)], psum[6][:, 0:36].unsqueeze(1),
                              rowv[:, W_RB:W_RB + 36].unsqueeze(1), ALU.add).then_inc(logits_saved.sem, 1)

        def e_vector(dve, tile, first, last):
            if first:
                e_save_y(dve, tile)
            e_residual(dve, tile, 0)
            if not last:
                e_save_y(dve, shifted(tile, 1))
            if not first:
                e_modulate(dve, shifted(tile, -1))
            e_residual(dve, tile, 1)
            if not first:
                e_save_logits(dve, shifted(tile, -1))
            if last:
                e_modulate(dve, tile)
                e_save_logits(dve, tile)

        rr = Region()
        r4 = [rr(NLAT, 4) for _ in range(6)]
        r8 = [rr(NLAT) for _ in range(26)]
        r32 = [rr(NLAT, 32) for _ in range(9)]
        rexp = rr(NLAT, 4)
        pre = rr(NLAT + 1, 32)
        rank = rr(NLAT, 32)
        cnt = [rr(32) for _ in range(8)]
        over = [rr(16, 32) for _ in range(3)]
        pool_go = sem("pool_go")
        route_step = Signal(sem("route_step"), 0, 109)
        exp_in = sem("exp_in")
        exp_out = sem("exp_out")
        ranks_in = sem("ranks_in")
        rank_done = sem("rank_done")
        addr_ready = sem("addr_ready")
        ids_in = sem("ids_in")
        scattered = sem("scattered")
        slots_in = sem("slots_in")
        ctl_ready = sem("ctl_ready")

        def r_vector(dve):
            step = Chain(dve, route_step, ones)

            def tt(out, a, b, op):
                step(dve.tensor_tensor(out, a, b, op))
                return out

            def ts(out, a, s1, op1, s2=None, op2=None):
                step(dve.tensor_scalar(out, a, s1, s2, op1, *([op2] if op2 else [])))
                return out

            def red(out, a, op):
                step(dve.tensor_reduce(out, a, AX.X, op))
                return out

            def b(v, n):
                return v.unsqueeze(2).to_broadcast([P, NLAT, n])

            logits_saved.wait(dve, e_tile(NLAT - 1), 1)
            glog, elog = logits[:, :, 0:4], logits[:, :, 4:36]
            far = 99.0
            iota4 = ts(cnt[0][:, 0:4], consts[:, I_G4:I_G4 + 4], far, ALU.subtract)
            iota32 = ts(cnt[1], consts[:, I_E32:I_E32 + 32], far, ALU.subtract)
            i4 = iota4.unsqueeze(1).to_broadcast([P, NLAT, 4])
            i32 = iota32.unsqueeze(1).to_broadcast([P, NLAT, 32])

            spare = list(r8[18:])

            def first_max(vals, n, iota, tmp):
                m = red(spare.pop(), vals, ALU.max)
                eq = tt(tmp[0], vals, b(m, n), ALU.is_equal)
                at = red(spare.pop(), tt(tmp[1], eq, iota, ALU.mult), ALU.min)
                return m, at, tt(tmp[0], iota, b(at, n), ALU.is_equal)

            gmax, _, goh = first_max(glog, 4, i4, r4[0:2])
            dve.tensor_tensor(r4[2], glog, b(gmax, 4), ALU.subtract).then_inc(exp_in, 1)
            em = r32[0]
            for g in range(4):
                sel = goh[:, :, g:g + 1].to_broadcast([P, NLAT, 8])
                tt(em[:, :, 8 * g:8 * g + 8], elog[:, :, 8 * g:8 * g + 8], sel, ALU.mult)
            pen = ts(r4[3], goh, 1.0, ALU.subtract, 1e30, ALU.mult)
            for g in range(4):
                tt(em[:, :, 8 * g:8 * g + 8], em[:, :, 8 * g:8 * g + 8], pen[:, :, g:g + 1].to_broadcast([P, NLAT, 8]),
                   ALU.add)
            v1, at1, oh1 = first_max(em, 32, i32, r32[1:3])
            away = ts(r32[3], oh1, -2e30, ALU.mult)
            em2 = tt(r32[3], away, em, ALU.add)
            v2, at2, oh2 = first_max(em2, 32, i32, [r32[4], r32[2]])
            dve.tensor_tensor(r8[0], v2, v1, ALU.subtract).then_inc(exp_in, 1)
            both = tt(r32[5], oh1, oh2, ALU.add)
            step(dve.memset(pre[:, 0], 0.0))
            for t in range(NLAT):
                tt(pre[:, t + 1], pre[:, t], both[:, t], ALU.add)
            dve.sem_inc(ranks_in, 1)
            dve.wait_ge(exp_out, 1)
            gw = r8[2]
            step(dve.reciprocal(gw, red(r8[1], rexp, ALU.add)))
            dve.wait_ge(exp_out, 2)
            e2 = r8[3]
            den = r8[4]
            step(dve.reciprocal(den, ts(r8[5], e2, 1.0, ALU.add)))
            w1 = tt(pairw[:, 0], den, gw, ALU.mult)
            tt(pairw[:, 1], e2, w1, ALU.mult)
            dve.wait_ge(rank_done, 1)
            step(dve.tensor_copy(rank, psum[6][:, 0:256].rearrange("p (t e) -> p t e", t=NLAT)))
            c = ts(cnt[2], psum[7][:, 0:32], 1.0, ALU.max, 1.0, ALU.subtract)
            ci = cnt[3].bitcast(I32)
            step(dve.tensor_copy(ci, c))
            ts(cnt[4].bitcast(I32), ci, 7, ALU.arith_shift_right)
            more = cnt[2]
            step(dve.tensor_copy(more, cnt[4].bitcast(I32)))
            cum, nxt = cnt[3], cnt[4]
            step(dve.tensor_copy(cum, more))
            for sh in (1, 2, 4, 8, 16):
                step(dve.tensor_copy(nxt[:, 0:sh], cum[:, 0:sh]))
                tt(nxt[:, sh:32], cum[:, sh:32], cum[:, 0:32 - sh], ALU.add)
                cum, nxt = nxt, cum
            base = tt(cnt[5], cum, more, ALU.subtract)
            bb = base.unsqueeze(1).to_broadcast([P, NLAT, 32])
            for k, (oh, at) in enumerate(((oh1, at1), (oh2, at2))):
                rk = red(r8[6], tt(r32[6], oh, rank, ALU.mult), ALU.add)
                ob = red(r8[7], tt(r32[7], oh, bb, ALU.mult), ALU.add)
                ri, qi, pi = (r8[n].bitcast(I32) for n in (8, 9, 10))
                step(dve.tensor_copy(ri, rk))
                ts(qi, ri, 7, ALU.arith_shift_right)
                ts(pi, ri, 127, ALU.bitwise_and)
                step(dve.tensor_copy(r8[11], qi))
                step(dve.tensor_copy(r8[12], pi))
                q, p = r8[11], r8[12]
                own = ts(r8[13], q, 0.0, ALU.is_equal)
                blk = ts(r8[14], tt(r8[14], ob, q, ALU.add), float(EXPERTS - 1), ALU.add)
                e = ts(r8[15], at, far, ALU.add)
                e = tt(r8[15], e, blk, ALU.subtract)
                e = tt(r8[15], e, own, ALU.mult)
                blk = tt(r8[14], blk, e, ALU.add)
                slot = tt(r8[16], ts(r8[16], p, float(NBLK), ALU.mult), blk, ALU.add)
                row = tt(r8[17], ts(r8[17], blk, float(P), ALU.mult), p, ALU.add)
                step(dve.tensor_copy(slot_at[:, k], slot))
                dve.tensor_copy(row_at[:, k], row).then_inc(addr_ready, 1)
            k16 = consts[:, I_E32:I_E32 + 16].unsqueeze(2).to_broadcast([P, 16, 32])
            b16 = base.unsqueeze(1).to_broadcast([P, 16, 32])
            c16 = cum.unsqueeze(1).to_broadcast([P, 16, 32])
            lo = tt(over[0], b16, k16, ALU.is_le)
            hi = tt(over[1], c16, k16, ALU.is_gt)
            tt(over[0], lo, hi, ALU.mult)
            tt(over[0], over[0], consts[:, I_E32:I_E32 + 32].unsqueeze(1).to_broadcast([P, 16, 32]), ALU.mult)
            oe = red(cnt[6][:, 0:16], over[0], ALU.add)
            step(dve.tensor_copy(ctl[:, 0:16], oe))
            dve.tensor_copy(ctl[:, NOVER + 1:NOVER + 2], cum[:, 31:32]).then_inc(ctl_ready, 1)
            step.close()

        def r_scalar(act):
            act.wait_ge(exp_in, 1)
            act.activation(rexp, r4[2], ACT.Exp).then_inc(exp_out, 1)
            act.wait_ge(exp_in, 2)
            act.activation(r8[3], r8[0], ACT.Exp).then_inc(exp_out, 1)

        def r_tensor(pe):
            pe.wait_ge(ranks_in, 1)
            pe.matmul(psum[6][:, 0:256], consts[:, I_TRI:I_TRI + P], r32[5].rearrange("p t e -> p (t e)"),
                      start=True, stop=False)
            pe.matmul(psum[6][:, 0:256], onesm[:, :], pre[:, 0:NLAT].rearrange("p t e -> p (t e)"),
                      start=False, stop=True)
            pe.matmul(psum[7][:, 0:32], onesm[:, :], pre[:, NLAT], start=True, stop=True).then_inc(rank_done, 1)

        def r_pool(pool):
            pool.wait_ge(ids_in, 32)
            for k in range(2):
                pool.wait_ge(addr_ready, k + 1)
                pool.sem_inc(pool_go, 1)
                for t in range(NLAT):
                    pool.indirect_dma_start(slots_d, bass.IndirectOffsetOnAxis(ap=slot_at[:, k, t:t + 1], axis=0),
                                            tokid[:, t:t + 1], None).then_inc(scattered, 16)

        def r_sync(sp):
            sp.wait_ge(scattered, 16 * 2 * NLAT)
            sp.dma_start(slots[:, :], slots_d.rearrange("(p b) a -> p (b a)", p=P)).then_inc(slots_in, 16)

        rm = Region(w_out_at)
        xg = rm(2, D)
        xT = [rm(KD, P) for _ in range(2)]
        sg = rm(HB, P)
        hid = rm(HB, P)
        ys = rm(2, D)
        col_ready = signal("col_ready", 1)
        rows_in_m = [sem("rows_in_m0"), sem("rows_in_m1")]
        m_turned = signal("m_turned", 2, 0, 1)
        xT_act = signal("xT_act", 4)
        xT_dve = signal("xT_dve", 4)
        gate_done = signal("gate_done", 1)
        mup_done = signal("mup_done", 1, 0, 1)
        silu_ready = signal("silu_ready", 1, 0, 1)
        hid_ready = signal("hid_ready", 1, 0, 1)
        down_done = signal("down_done", 2)
        ys_act = signal("ys_act", 1, 0, 1)
        ys_dve = signal("ys_dve", 1, 0, 1)
        blk_out = [sem("blk_out0"), sem("blk_out1")]
        experts_done = sem("experts_done")

        def block_over(k):
            return Tile(False, 0, k + EXPERTS, k + EXPERTS // 2, 0)

        def after(tile, over):
            if over:
                return Tile(False, 0, tile.lat_before + 1, tile.pair + 1, 0)
            return shifted(tile, 1)

        def m_sync(sp, tile, over, expert):
            def wait_used(n):
                if n == 0:
                    gate_done.wait(sp, tile, 0 if over else -1)
                elif n == 1:
                    mup_done.wait(sp, tile, 0 if over else -1)
                else:
                    down_done.wait(sp, tile, 0 if over else -2)

            moe_load(sp, expert, tile.slot, wait_used)

        def m_fetch(pool, tile, over):
            col_ready.wait(pool, tile, 2 if over else 1)
            m_turned.wait(pool, tile, 0 if over else -2)
            pool.sem_inc(pool_go, 1)
            pool.indirect_dma_start(xg[:, tile.slot], None, normed,
                                    bass.IndirectOffsetOnAxis(ap=idxc[:, tile.slot:tile.slot + 1], axis=0)
                                    ).then_inc(rows_in_m[tile.slot], 16)

        def m_turn(pe, tile):
            pe.wait_ge(rows_in_m[tile.slot], 16 * (tile.pair + 1))
            xT_act.wait_before(pe, tile)
            xT_dve.wait_before(pe, tile)
            for half in range(2):
                for j in range(4):
                    k = 4 * half + j
                    mm = pe.transpose(psum[2 + half][:, P * j:P * (j + 1)], xg[:, tile.slot, P * k:P * (k + 1)], ident)
                mm.then_inc(m_turned.sem, 1)

        def m_tensor(pe, tile, over):
            s = tile.slot
            uses = tile.pair + 1

            def up(bank, w):
                for hb in range(HB):
                    for k in range(KD):
                        mm = pe.matmul(bank[:, P * hb:P * (hb + 1)], w[:, k, P * hb:P * (hb + 1)], xT[s][:, k],
                                       start=(k == 0), stop=(k == KD - 1))
                return mm

            xT_act.wait_all(pe, tile)
            xT_dve.wait_all(pe, tile)
            pe.wait_ge(moe_in[s][0], 16 * uses)
            silu_ready.wait_before(pe, tile)
            up(psum[0], wg[s]).then_inc(gate_done.sem, 1)
            pe.wait_ge(moe_in[s][1], 16 * uses)
            hid_ready.wait_before(pe, tile)
            up(psum[1], wu[s]).then_inc(mup_done.sem, 1)
            m_turn(pe, after(tile, over))
            pe.wait_ge(moe_in[s][2], 16 * uses)
            hid_ready.wait_all(pe, tile)
            for half in range(2):
                (ys_act, ys_dve)[half].wait_before(pe, tile)
                for hb in range(HB):
                    mm = pe.matmul(psum[4 + half], hid[:, hb], wd[s][:, hb, 512 * half:512 * half + 512],
                                   start=(hb == 0), stop=(hb == HB - 1))
                mm.then_inc(down_done.sem, 1)

        def m_modulate_scalar(act, tile, over):
            mup_done.wait(act, tile, 0 if over else -1)
            for k in range(4):
                m_turned.wait(act, tile, 1)
                act.activation(xT[tile.slot][:, k], psum[2][:, P * k:P * (k + 1)], ACT.Identity,
                               scale=scale2[:, k:k + 1], bias=modc[:, 24 + k, 0:1]).then_inc(xT_act.sem, 1)

        def m_modulate_vector(dve, tile, over):
            mup_done.wait(dve, tile, 0 if over else -1)
            for k in range(4, 8):
                m_turned.wait(dve, tile, 2)
                dve.tensor_scalar(xT[tile.slot][:, k], psum[3][:, P * (k - 4):P * (k - 3)],
                                  scale2[:, k:k + 1], modc[:, 24 + k, 0:1], ALU.mult, ALU.add
                                  ).then_inc(xT_dve.sem, 1)

        def m_scalar(act, tile, over):
            s = tile.slot
            gate_done.wait(act, tile, 1)
            hid_ready.wait_before(act, tile)
            act.activation(sg, psum[0].rearrange("p (a b) -> p a b", a=HB), ACT.Silu).then_inc(silu_ready.sem, 1)
            m_modulate_scalar(act, after(tile, over), over)
            down_done.wait(act, tile, 1)
            act.wait_ge(blk_out[s], 16 * tile.pair + 16)
            act.activation(ys[:, s, 0:512], psum[4], ACT.Copy).then_inc(ys_act.sem, 1)
            ys_act.wait_all(act, tile)
            ys_dve.wait_all(act, tile)
            act.dma_start(expert_out.rearrange("(b p) c -> b p c", p=P)[ds(tile.lat_before, 1)]
                          .rearrange("a p c -> p (a c)"), ys[:, s]).then_inc(blk_out[s], 16)

        def m_column(dve, tile, over):
            dve.tensor_copy(idxc[:, tile.slot:tile.slot + 1], slots[:, ds(tile.lat_before, 1)]
                            ).then_inc(col_ready.sem, 1)

        def m_vector(dve, tile, over):
            s = tile.slot
            mup_done.wait(dve, tile, 1)
            silu_ready.wait_all(dve, tile)
            dve.tensor_tensor(hid, psum[1].rearrange("p (a b) -> p a b", a=HB), sg, ALU.mult).then_inc(hid_ready.sem, 1)
            m_modulate_vector(dve, after(tile, over), over)
            m_column(dve, after(after(tile, over), over), over)
            down_done.wait(dve, tile, 2)
            dve.wait_ge(blk_out[s], 16 * tile.pair + 16)
            dve.tensor_copy(ys[:, s, 512:1024], psum[5]).then_inc(ys_dve.sem, 1)

        def over_loop(eng, body):
            eng.wait_ge(ctl_ready, 1)
            count = eng.value_load(ctl[0:1, NOVER + 1:NOVER + 2], min_val=0, max_val=NOVER)
            with eng.Fori(0, count) as k:
                body(eng, block_over(k), k)

        def m_blocks(eng, body, from_pair=0):
            with eng.Fori(from_pair, EXPERTS // 2) as i:
                for slot in range(2):
                    body(eng, latent_tile(i, slot), False)

        def m_all_sync(sp):
            m_blocks(sp, lambda e, tile, over: m_sync(e, tile, over, tile.lat_before), 1)
            sp.wait_ge(ctl_ready, 1)

            def extra(e, tile, k):
                expert = e.value_load(ctl[0:1, ds(k, 1)], min_val=0, max_val=EXPERTS - 1)
                m_sync(e, tile, True, expert)

            over_loop(sp, extra)

        def m_all_pool(pool):
            pool.wait_ge(n2_out, 16 * (NLAT + 1))
            m_fetch(pool, e_tile(0), False)
            m_blocks(pool, lambda e, tile, over: m_fetch(e, shifted(tile, 1), over))
            over_loop(pool, lambda e, tile, k: m_fetch(e, after(tile, True), True))

        def m_all_tensor(pe):
            m_turn(pe, e_tile(0))
            m_blocks(pe, m_tensor)
            over_loop(pe, lambda e, tile, k: m_tensor(e, tile, True))

        def m_all_scalar(act):
            m_modulate_scalar(act, e_tile(0), False)
            m_blocks(act, m_scalar)
            for s in range(2):
                act.wait_ge(blk_out[s], 16 * (EXPERTS // 2 + 1))

            def extra(e, tile, k):
                m_scalar(e, tile, True)
                e.wait_ge(blk_out[0], 16 * tile.pair + 32)

            act.wait_ge(spare_out, 16)
            over_loop(act, extra)
            act.sem_inc(experts_done, 1)

        def m_all_vector(dve):
            dve.wait_ge(slots_in, 16)
            m_column(dve, e_tile(0), False)
            m_column(dve, e_tile(1), False)
            m_modulate_vector(dve, e_tile(0), False)
            m_blocks(dve, m_vector)
            m_turned.wait(dve, block_over(0), 2)
            dve.tensor_copy(idxc[:, 0:1], slots[:, EXPERTS + 1:EXPERTS + 2]).then_inc(col_ready.sem, 1)
            over_loop(dve, lambda e, tile, k: m_vector(e, tile, True))

        rg = Region(rr.at)
        gx = rg(2, D)
        gy = rg(2, 2, D)
        assert rg.at <= expert_at
        ga = rg(2, D)
        gb = rg(D)
        x2 = rg(2, D)
        gn = rg(D)
        go = rg(2, D)
        gstat = rg(16)
        gw_c = rg(2, 2)
        gx_in = [sem("gx_in0"), sem("gx_in1")]
        gy_in = [sem("gy_in0"), sem("gy_in1")]
        gcol = signal("gcol", 2)
        ga_ready = signal("ga_ready", 1)
        gb_steps = signal("gb_steps", 2)
        x2_ready = signal("x2_ready", 1, 0, 1)
        g_sq = signal("g_sq", 1)
        g_rstd = signal("g_rstd", 3)
        gn_ready = signal("gn_ready", 1, 0, 1)
        go_ready = signal("go_ready", 1, 0, 1)
        out_done = [sem("out_done0"), sem("out_done1")]

        def g_load(sp, tile):
            sp.dma_start(gx[:, tile.slot], resid[ds(tile.lat_before, 1)].rearrange("a p c -> p (a c)")
                         ).then_inc(gx_in[tile.slot], 16)

        def g_store(sp, tile):
            go_ready.wait_all(sp, tile)
            sp.dma_start(out.rearrange("a (t p) d -> t p (a d)", p=P)[ds(tile.lat_before, 1)]
                         .rearrange("a p c -> p (a c)"), go[:, tile.slot]).then_inc(out_done[tile.slot], 16)

        def g_sync(sp):
            for slot in range(2):
                sp.wait_ge(x1_out[slot], 16 * (NLAT // 2 + 1))
            for slot in range(2):
                g_load(sp, e_tile(slot))
            with sp.Fori(0, NLAT // 2 - 1) as i:
                for slot in range(2):
                    g_store(sp, latent_tile(i, slot))
                    g_load(sp, latent_tile(i + 1, slot))
            for slot in range(2):
                g_store(sp, latent_tile(NLAT // 2 - 1, slot))
            for slot in range(2):
                sp.wait_ge(out_done[slot], 16 * (NLAT // 2 + 1))

        def g_columns(dve, tile):
            s, t = tile.slot, tile.lat_before
            dve.tensor_copy(gidx[:, s].unsqueeze(2), row_at[:, :, ds(t, 1)]).then_inc(gcol.sem, 1)
            dve.tensor_copy(gw_c[:, s].unsqueeze(2), pairw[:, :, ds(t, 1)]).then_inc(gcol.sem, 1)

        def two_on(tile):
            return shifted(shifted(tile, 1), 1)

        def g_fetch(pool, tile, first=False):
            gcol.wait_all(pool, tile)
            if not first:
                x2_ready.wait(pool, tile, -1)
            pool.sem_inc(pool_go, 1)
            for k in range(2):
                pool.indirect_dma_start(gy[:, tile.slot, k], None, expert_out,
                                        bass.IndirectOffsetOnAxis(ap=gidx[:, tile.slot, k:k + 1], axis=0)
                                        ).then_inc(gy_in[tile.slot], 16)

        def g_pool(pool, tile, behind):
            if behind > 1:
                g_fetch(pool, two_on(tile))
            rstd_pool(pool, tile, gstat, g_sq, g_rstd)
            gn_ready.wait_all(pool, tile)
            pool.wait_ge(out_done[tile.slot], 16 * tile.pair + 16)
            pool.tensor_tensor(go[:, tile.slot], gn, rowv[:, W_FN:W_FN + D], ALU.mult).then_inc(go_ready.sem, 1)

        def g_first(act, tile):
            s = tile.slot
            x2_ready.wait(act, tile, -1)
            act.wait_ge(gy_in[s], 32 * (tile.pair + 1))
            gcol.wait_all(act, tile)
            act.activation(ga[:, s], gy[:, s, 0], ACT.Copy, scale=gw_c[:, s, 0:1]).then_inc(ga_ready.sem, 1)

        def g_scalar(act, tile, behind):
            s = tile.slot
            if behind:
                g_first(act, shifted(tile, 1))
            x2_ready.wait_all(act, tile)
            go_ready.wait_before(act, tile)
            act.activation(gn, x2[:, s], ACT.Square, accum_out=gstat[:, 0:1]).then_inc(g_sq.sem, 1)
            g_rstd.wait(act, tile, 3)
            act.activation(gn, x2[:, s], ACT.Copy, scale=gstat[:, 3:4]).then_inc(gn_ready.sem, 1)

        def g_vector(dve, tile, behind):
            s = tile.slot
            gn_ready.wait(dve, tile, -1)
            dve.wait_ge(gy_in[s], 32 * (tile.pair + 1))
            dve.wait_ge(gx_in[s], 16 * (tile.pair + 1))
            ga_ready.wait_all(dve, tile)
            x2_ready.wait_before(dve, tile)
            dve.scalar_tensor_tensor(gb, gy[:, s, 1], gw_c[:, s, 1:2], ga[:, s], ALU.mult, ALU.add).then_inc(gb_steps.sem, 1)
            gb_steps.wait(dve, tile, 1)
            dve.tensor_tensor(gb, gb, g2row[:, :], ALU.mult).then_inc(gb_steps.sem, 1)
            gb_steps.wait(dve, tile, 2)
            dve.tensor_tensor(x2[:, s], gb, gx[:, s], ALU.add).then_inc(x2_ready.sem, 1)
            if behind > 1:
                g_columns(dve, two_on(tile))

        def g_tiles(eng, body):
            with eng.Fori(0, NLAT // 2 - 1) as i:
                for slot in range(2):
                    body(eng, latent_tile(i, slot), 2)
            body(eng, e_tile(NLAT - 2), 1)
            body(eng, e_tile(NLAT - 1), 0)

        block = ctx.enter_context(nc.Block())

        def each_pair(eng, body, tile_of):
            with eng.Fori(0, NLAT // 2) as i:
                for slot in range(2):
                    body(eng, tile_of(i, slot))

        @block.sync
        def _(sp):
            a_sync(sp)
            for tile in ctx_tiles():
                b_sync(sp, tile)
            each_pair(sp, b_sync, projection_tile)
            sp.sem_inc(y_out.sem, y_out.base)
            d_sync(sp)
            for count in (x1_out[0], x1_out[1], n2_out, out_done[0], out_done[1]):
                sp.sem_inc(count, 16)
            e_sync(sp)
            r_sync(sp)
            m_all_sync(sp)
            g_sync(sp)

        @block.tensor
        def _(pe):
            a_tensor(pe)
            b_prep_tensor(pe, ctx_tiles()[0])
            for tile in ctx_tiles():
                b_tensor(pe, tile)
            each_pair(pe, b_tensor, projection_tile)
            pe.sem_inc(t_done.sem, t_done.base)
            pe.sem_inc(av_done.sem, av_done.base)
            pe.wait_ge(kv_in[0], 16)
            each_pair(pe, d_tensor, latent_tile)
            for done in (n2_turned, routed, m_turned, mup_done):
                pe.sem_inc(done.sem, done.base)
            e_rows_tensor(pe)
            skewed(pe, e_tensor)
            r_tensor(pe)
            m_all_tensor(pe)

        @block.scalar
        def _(act):
            a_scalar(act)
            b_prep_scalar(act, ctx_tiles()[0])
            for tile in ctx_tiles():
                b_scalar(act, tile)
            each_pair(act, b_scalar, projection_tile)
            act.sem_inc(pt_act.sem, pt_act.base)
            each_pair(act, d_scalar, latent_tile)
            for done in (n2_ready, silu_ready, ys_act, gn_ready):
                act.sem_inc(done.sem, done.base)
            for count in blk_out:
                act.sem_inc(count, 16)
            act.wait_ge(y_out.sem, 16 * (NLAT + 1))
            act.wait_ge(e_weights_in, 48)
            for slot in range(2):
                act.wait_ge(e_in[slot], 32)
            for slot in range(2):
                moe_load(act, slot, slot)
            each_pair(act, e_scalar, latent_tile)
            r_scalar(act)
            m_all_scalar(act)
            g_first(act, e_tile(0))
            g_tiles(act, g_scalar)

        @block.gpsimd
        def _(pool):
            pool.wait_ge(halfs_ready, 1)
            pool.wait_ge(decay_exp, 14)
            pool.sem_inc(qfb_ready.sem, qfb_ready.base)
            b_prep_pool(pool, ctx_tiles()[0])
            for tile in ctx_tiles():
                b_pool(pool, tile)
            each_pair(pool, b_pool, projection_tile)
            for n in range(3):
                pool.wait_ge(kv_in[n], 16)
            scan_states(pool, 0, 64, (0, 1), list(range(NLAT)), fwd_state)
            scan_states(pool, 64, 128, (1, 0), list(range(NLAT - 1, -1, -1)), bwd_state)
            each_pair(pool, d_pool, latent_tile)
            pool.sem_inc(go_ready.sem, go_ready.base)
            each_pair(pool, e_pool, latent_tile)
            r_pool(pool)
            m_all_pool(pool)
            pool.wait_ge(experts_done, 1)
            g_fetch(pool, e_tile(0), True)
            g_fetch(pool, e_tile(1), True)
            g_tiles(pool, g_pool)

        @block.vector
        def _(dve):
            a_vector(dve)
            dve.sem_inc(rot.sem, rot.base)
            b_prep_vector(dve, ctx_tiles()[0])
            for tile in ctx_tiles():
                b_vector(dve, tile)
            each_pair(dve, b_vector, projection_tile)
            for done in (pt_dve, o_saved, a_ready, ret_saved, y_ready, fin):
                dve.sem_inc(done.sem, done.base)
            each_pair(dve, d_vector, latent_tile)
            for done in (h2_ready, logits_saved, hid_ready, ys_dve, x2_ready):
                dve.sem_inc(done.sem, done.base)
            e_rows_vector(dve)
            skewed(dve, e_vector)
            r_vector(dve)
            m_all_vector(dve)
            g_columns(dve, e_tile(0))
            g_columns(dve, e_tile(1))
            g_tiles(dve, g_vector)


_OUTS = [((1, SEQ, D), "float32")]


def _column_orders():
    swa, diff, ret, mla = 0, 512, 1280, 2304
    span = lambda lo, n: np.arange(lo, lo + n)
    swa_q = np.concatenate([span(swa + 64 * h, 64) for h in (0, 2, 1, 3)])
    order = np.concatenate([
        span(mla + 256, 128), span(mla + 384, 32), span(mla, 256),
        span(swa + 256, 128), span(ret + 256, 256), swa_q, span(ret, 256),
        span(diff + 256, 256), span(diff, 256), span(swa + 384, 128), span(diff + 512, 256),
        span(ret + 512, 256), span(ret + 768, 256)])
    kv = np.arange(512).reshape(4, 128)
    return order, np.concatenate([kv[:, :64].ravel(), kv[:, 64:].ravel()])


def _constants():
    i = np.arange(P, dtype=np.float32)
    rel = i[None, :] - i[:, None]
    steps = np.stack([i + 1, P - i, P - 1 - i, i], 1)
    consts = np.concatenate([
        np.eye(P), np.maximum(rel, 0), np.maximum(-rel, 0), rel >= 0, rel <= 0, rel > 0, steps,
        np.broadcast_to(np.arange(32), (P, 32)), np.broadcast_to(np.arange(4), (P, 4))], 1).astype(np.float32)
    t = np.arange(SEQ)
    pos = np.stack([t // GRID_W, t % GRID_W], 1).astype(np.float32)
    parts = []
    for nf in (16, 8):
        inv = (1.0 / (np.float32(10000.0) ** (np.arange(nf, dtype=np.float32) / np.float32(nf)))).astype(np.float32)
        ang = pos[:, :, None] * inv
        cos, sin = np.cos(ang), np.sin(ang)
        parts += [np.concatenate([cos, cos], 2).reshape(SEQ, -1), sin.reshape(SEQ, -1), (-sin).reshape(SEQ, -1)]
    tables = np.concatenate(parts, 1).astype(np.float32).reshape(NLAT, P, T_END)
    q, k = i[:, None], i[None, :]
    mask = np.zeros((NLAT, P, 2, P), np.float32)
    mask[:, :, 0] = np.where(q - (k - P) <= WINDOW, 0, NEG)
    mask[:, :, 1] = np.where((k + P) - q <= WINDOW, 0, NEG)
    mask[0, :, 0] = NEG
    mask[-1, :, 1] = NEG
    return consts, tables, mask.reshape(NLAT, P, 2 * P)


def kernel(**inputs):
    import concourse.bacc as _bacc
    from concourse.bass_utils import run_bass_kernel_spmd as _run

    a = {k: np.ascontiguousarray(v) for k, v in inputs.items()}
    order, kv_order = _column_orders()
    consts, tables, mask = _constants()
    row = lambda *names: [a[n].reshape(-1, P) for n in names]
    arrays = {
        "tokens": np.concatenate([a["ctx"][0], a["x"][0], a["ctx"][0][:P]], 0).reshape(NTOK + 1, P, D),
        "x": a["x"],
        "cols": np.concatenate(row("c", "c_ctx", "b_mod", "norm1_g", "norm2_g", "mla_q_norm_g", "mla_kv_norm_g"), 0),
        "rows": np.concatenate([a[n].reshape(-1) for n in ("diff_subln_g", "ret_gn_g", "swa_sink", "ret_decay_logit")]
                               + [a["diff_lambda"][0, 0], a["diff_lambda"][0, 2], a["diff_lambda"][0, 1],
                                  a["diff_lambda"][0, 3]]
                               + [a[n].reshape(-1) for n in ("moe_b_group", "moe_b_expert", "final_norm_g")])[None],
        "w_mod": a["w_mod"],
        "w_in": np.ascontiguousarray(a["w_in"][:, :, order]),
        "w_uq": a["mla_w_uq"],
        "w_ukv": np.ascontiguousarray(a["mla_w_ukv"][:, :, kv_order]),
        "w_out": a["w_out"],
        "w_route": np.concatenate([a["moe_w_group"][0], a["moe_w_expert"][0]], 1),
        "w_gate": a["moe_w_gate"][0],
        "w_up": a["moe_w_up"][0],
        "w_down": a["moe_w_down"][0],
        "consts": consts,
        "tables": tables,
        "mask": mask,
        "ids": np.concatenate([np.arange(SEQ, dtype=np.int32).reshape(NLAT, P).T, np.zeros((P, NBLK), np.int32)], 1),
        "zeros": np.zeros((P, D), np.float32),
    }
    nc = _bacc.Bacc("TRN2", target_bir_lowering=False, num_devices=1)
    A = {n: nc.dram_tensor(n, v.shape, mybir.dt.from_np(v.dtype), kind="ExternalInput").ap()
         for n, v in arrays.items()}
    outs = [nc.dram_tensor(f"out_{i}", shape, mybir.dt.from_np(np.dtype(dt)), kind="ExternalOutput").ap()
            for i, (shape, dt) in enumerate(_OUTS)]
    build(nc, A, *outs)
    r = _run(nc, [arrays], core_ids=[0])
    got = tuple(r.results[0][f"out_{i}"] for i in range(len(_OUTS)))
    return got[0]
```
